# Optimizing a Trainium2 kernel written in Bass

```python
import jax
import jax.numpy as jnp
from jax import lax
import numpy as np

D_MODEL = 1024
BATCH = 1
SEQ = 1024
DEPTH = 2
DEC_BATCH = 8
DEC_SEQ = 16
PAST_LEN = 256

CHUNK = 64
Q_BLOCK = 128
EPS = 1e-6
HEAD_DIM = 64
N_GROUPS = 4
GROUP_WIDTH = D_MODEL // N_GROUPS
MIX_WIDTH = N_GROUPS * GROUP_WIDTH
N_HEADS = GROUP_WIDTH // HEAD_DIM
ROT_DIM = HEAD_DIM // 4
ROPE_THETA = 500000.0
A_BAND = 8 * CHUNK
REL_CLIP = 128
MLA_Q_LORA = 384
MLA_KV_LORA = 128
MLA_NOPE = 64
MLA_ROPE = 32
MLA_V = HEAD_DIM
IDX_HEADS = 8
IDX_DIM = 32
DSA_TOPK = 256
FORGET_BIAS = 3.0
PLE_DIM = 256
N_QK_GAINS = 8

IN_SPLITS = (
    ('a_q', N_HEADS * HEAD_DIM), ('a_k', N_HEADS * HEAD_DIM), ('a_v', N_HEADS * HEAD_DIM), ('a_g', GROUP_WIDTH),
    ('b_cq', MLA_Q_LORA), ('b_ckv', MLA_KV_LORA), ('b_kr', MLA_ROPE), ('b_g', GROUP_WIDTH),
    ('c_q', N_HEADS * HEAD_DIM), ('c_k', HEAD_DIM), ('c_v', HEAD_DIM), ('c_iq', IDX_HEADS * IDX_DIM),
    ('c_ik', IDX_DIM), ('c_iw', IDX_HEADS), ('c_g', GROUP_WIDTH),
    ('d_q', N_HEADS * HEAD_DIM), ('d_k', N_HEADS * HEAD_DIM), ('d_v', N_HEADS * HEAD_DIM), ('d_f', N_HEADS), ('d_g', GROUP_WIDTH),
)
IN_WIDTH = sum(n for _, n in IN_SPLITS)

kernel_name = 'hybrid_streaming_encoder_step'

def rms_norm(x, g):
    xf = x.astype(jnp.float32)
    y = xf * lax.rsqrt(jnp.mean(jnp.square(xf), axis=-1, keepdims=True) + EPS)
    return (y * g.astype(jnp.float32)).astype(x.dtype)

def split_heads(t, n):
    return t.reshape(t.shape[:-1] + (n, t.shape[-1] // n))

def split_columns(z):
    out, off = {}, 0
    for name, n in IN_SPLITS:
        out[name] = z[..., off:off + n]
        off += n
    return out

def rotary(x, pos, rot_dim):
    half = rot_dim // 2
    inv = jnp.float32(ROPE_THETA) ** (-jnp.arange(half, dtype=jnp.float32) / half)
    ang = pos.astype(jnp.float32)[:, None] * inv[None, :]
    cos = jnp.cos(ang)[None, :, None, :]
    sin = jnp.sin(ang)[None, :, None, :]
    xr = x[..., :rot_dim].astype(jnp.float32)
    x1, x2 = xr[..., :half], xr[..., half:]
    rot = jnp.concatenate([x1 * cos - x2 * sin, x2 * cos + x1 * sin], axis=-1).astype(x.dtype)
    return jnp.concatenate([rot, x[..., rot_dim:]], axis=-1)

def masked_softmax(s, mask):
    return jax.nn.softmax(jnp.where(mask, s.astype(jnp.float32), -jnp.inf), axis=-1)

def sweep_query_blocks(fn, q_pos, *q_side):
    T = q_pos.shape[0]
    blk = min(Q_BLOCK, T)
    nb = T // blk
    qs = tuple(jnp.moveaxis(a.reshape((a.shape[0], nb, blk) + a.shape[2:]), 1, 0) for a in q_side)
    out = lax.map(lambda args: fn(*args), (q_pos.reshape(nb, blk),) + qs)
    out = jnp.moveaxis(out, 0, 1)
    return out.reshape((out.shape[0], T) + out.shape[3:])

def chunk_band_attention(q, k, v, past_k, past_v, rel_bias):
    B, T, H, Dh = q.shape
    Pa = past_k.shape[1]
    n_chunks = -(-T // CHUNK)
    pad = n_chunks * CHUNK - T
    width = A_BAND + CHUNK

    def band_source(new, past):
        front = jnp.zeros((B, A_BAND - Pa, H, Dh), new.dtype)
        back = jnp.zeros((B, pad, H, Dh), new.dtype)
        return jnp.concatenate([front, past.astype(new.dtype), new, back], axis=1)

    band_idx = jnp.arange(n_chunks)[:, None] * CHUNK + jnp.arange(width)[None, :]
    kb = band_source(k, past_k)[:, band_idx]
    vb = band_source(v, past_v)[:, band_idx]
    valid = (band_idx >= A_BAND - Pa) & (band_idx < A_BAND + T)
    qc = jnp.pad(q, ((0, 0), (0, pad), (0, 0), (0, 0))).reshape(B, n_chunks, CHUNK, H, Dh)
    rel = jnp.clip(jnp.arange(CHUNK)[:, None] + A_BAND - jnp.arange(width)[None, :], -REL_CLIP, REL_CLIP) + REL_CLIP
    bias = rel_bias.astype(jnp.float32)[:, rel]
    s = jnp.einsum('bcqhd,bckhd->bchqk', qc, kb).astype(jnp.float32) * Dh ** -0.5 + bias[None, None]
    p = masked_softmax(s, valid[None, :, None, None, :])
    o = jnp.einsum('bchqk,bckhd->bcqhd', p.astype(v.dtype), vb)
    return o.reshape(B, n_chunks * CHUNK, H, Dh)[:, :T]

def latent_attention(q_nope, q_rope, q_pos, k_nope, k_rope, v, k_pos):
    scale = (MLA_NOPE + MLA_ROPE) ** -0.5
    k_chunk = k_pos // CHUNK

    def block(qp, qn, qr):
        s = (jnp.einsum('bqhd,bkhd->bhqk', qn, k_nope) + jnp.einsum('bqhr,bkr->bhqk', qr, k_rope)).astype(jnp.float32) * scale
        p = masked_softmax(s, k_chunk[None, :] <= (qp // CHUNK)[:, None])
        return jnp.einsum('bhqk,bkhd->bqhd', p.astype(v.dtype), v)

    return sweep_query_blocks(block, q_pos, q_nope, q_rope)

def indexed_sparse_attention(q, iq, iw, q_pos, k, v, ik, k_pos, k_sel):
    k_chunk = k_pos // CHUNK

    def block(qp, qb, iqb, iwb):
        logits = jnp.einsum('bqhd,bkd->bqhk', iqb, ik).astype(jnp.float32) * IDX_DIM ** -0.5
        score = jnp.einsum('bqh,bqhk->bqk', iwb.astype(jnp.float32) * IDX_HEADS ** -0.5, jax.nn.relu(logits))
        admissible = k_chunk[None, :] <= (qp // CHUNK)[:, None]
        score = jnp.where(admissible[None], score, -jnp.inf)
        top_val, top_idx = lax.top_k(score, k_sel)
        kg = jax.vmap(lambda kk, ii: kk[ii])(k, top_idx)
        vg = jax.vmap(lambda vv, ii: vv[ii])(v, top_idx)
        s = jnp.einsum('bqhd,bqkd->bhqk', qb, kg).astype(jnp.float32) * HEAD_DIM ** -0.5
        p = masked_softmax(s, jnp.isfinite(top_val)[:, None])
        return jnp.einsum('bhqk,bqkd->bqhd', p.astype(v.dtype), vg)

    return sweep_query_blocks(block, q_pos, q, iq, iw)

def forgetting_attention(q, q_pos, f_q, k, v, f_k, k_pos):
    scale = HEAD_DIM ** -0.5
    f_kt = jnp.moveaxis(f_k, 2, 1)

    def block(qp, qb, fqb):
        s = jnp.einsum('bqhd,bkhd->bhqk', qb, k).astype(jnp.float32) * scale
        s = s + jnp.moveaxis(fqb, 2, 1)[..., None] - f_kt[:, :, None, :]
        p = masked_softmax(s, k_pos[None, :] <= qp[:, None])
        return jnp.einsum('bhqk,bkhd->bqhd', p.astype(v.dtype), v)

    return sweep_query_blocks(block, q_pos, q, f_q)

def trunk_layer(x, p, past, w):
    pa_k, pa_v, pb_ckv, pb_kr, pc_k, pc_v, pc_ik, pd_k, pd_v, pd_lf = past
    B, T, _ = x.shape
    P = pb_ckv.shape[1]
    q_pos = P + jnp.arange(T)
    k_pos = jnp.arange(P + T)
    g = w['g_qk']
    cat = lambda a, b: jnp.concatenate([a.astype(b.dtype), b], axis=1)
    z = split_columns(rms_norm(x, w['g_in']) @ w['w_in'])

    a_q = rms_norm(split_heads(z['a_q'], N_HEADS), g[0])
    a_k = rms_norm(split_heads(z['a_k'], N_HEADS), g[1])
    a_v = split_heads(z['a_v'], N_HEADS)
    y_a = chunk_band_attention(a_q, a_k, a_v, pa_k, pa_v, w['a_rel_bias'])

    cq = rms_norm(z['b_cq'], w['b_g_cq'])
    qb = split_heads(cq @ w['b_w_uq'], N_HEADS)
    qb_nope = rms_norm(qb[..., :MLA_NOPE], g[6])
    qb_rope = rotary(rms_norm(qb[..., MLA_NOPE:], w['g_rope'][0]), q_pos, MLA_ROPE)
    b_ckv = rms_norm(z['b_ckv'], w['b_g_ckv'])
    b_kr = rotary(rms_norm(z['b_kr'], w['g_rope'][1])[:, :, None], q_pos, MLA_ROPE)[:, :, 0]
    kr_all = cat(pb_kr, b_kr)
    kv = split_heads(cat(pb_ckv, b_ckv) @ w['b_w_ukv'], N_HEADS)
    kb_nope = rms_norm(kv[..., :MLA_NOPE], g[7])
    y_b = latent_attention(qb_nope, qb_rope, q_pos, kb_nope, kr_all, kv[..., MLA_NOPE:], k_pos)

    c_q = rotary(rms_norm(split_heads(z['c_q'], N_HEADS), g[2]), q_pos, ROT_DIM)
    c_k = rotary(rms_norm(z['c_k'], g[3])[:, :, None], q_pos, ROT_DIM)[:, :, 0]
    c_v = z['c_v']
    c_ik = z['c_ik']
    k_sel = min(DSA_TOPK, (P + T) // 4)
    y_c = indexed_sparse_attention(c_q, split_heads(z['c_iq'], IDX_HEADS), z['c_iw'], q_pos,
                                   cat(pc_k, c_k), cat(pc_v, c_v), cat(pc_ik, c_ik), k_pos, k_sel)

    d_q = rms_norm(split_heads(z['d_q'], N_HEADS), g[4])
    d_k = rms_norm(split_heads(z['d_k'], N_HEADS), g[5])
    d_v = split_heads(z['d_v'], N_HEADS)
    d_lf = jax.nn.log_sigmoid(z['d_f'].astype(jnp.float32) + w['d_b_f'].astype(jnp.float32))
    f_cum = jnp.cumsum(cat(pd_lf, d_lf), axis=1)
    y_d = forgetting_attention(d_q, q_pos, f_cum[:, P:], cat(pd_k, d_k), cat(pd_v, d_v), f_cum, k_pos)

    mix = jnp.concatenate([
        y_a.reshape(B, T, GROUP_WIDTH) * jax.nn.silu(z['a_g']),
        y_b.reshape(B, T, GROUP_WIDTH) * jax.nn.silu(z['b_g']),
        y_c.reshape(B, T, GROUP_WIDTH) * jax.nn.silu(z['c_g']),
        y_d.reshape(B, T, GROUP_WIDTH) * jax.nn.silu(z['d_g']),
    ], axis=-1).astype(x.dtype)
    x = x + mix @ w['w_out']
    x = x + jax.nn.sigmoid(rms_norm(x, w['g_ple']) @ w['w_ple_gate']) * (p @ w['w_ple_proj'])
    return x, (a_k, a_v, b_ckv, b_kr, c_k, c_v, c_ik, d_k, d_v, d_lf)

def setup_inputs(seed: int = 0) -> dict:
    key = jax.random.key(seed)
    ks = iter(jax.random.split(key, 40))

    def nrm(shape, scale=1.0):
        return scale * jax.random.normal(next(ks), shape, jnp.float32)

    a_past = min(A_BAND, PAST_LEN)
    return {
        'x_prompt': nrm((BATCH, SEQ, D_MODEL)),
        'x_sample': nrm((DEC_BATCH, DEC_SEQ, D_MODEL)),
        'cache_a_k': nrm((DEPTH, DEC_BATCH, a_past, N_HEADS, HEAD_DIM)),
        'cache_a_v': nrm((DEPTH, DEC_BATCH, a_past, N_HEADS, HEAD_DIM)),
        'cache_b_ckv': nrm((DEPTH, DEC_BATCH, PAST_LEN, MLA_KV_LORA)),
        'cache_b_krope': nrm((DEPTH, DEC_BATCH, PAST_LEN, MLA_ROPE)),
        'cache_c_k': nrm((DEPTH, DEC_BATCH, PAST_LEN, HEAD_DIM)),
        'cache_c_v': nrm((DEPTH, DEC_BATCH, PAST_LEN, HEAD_DIM)),
        'cache_c_idx_k': nrm((DEPTH, DEC_BATCH, PAST_LEN, IDX_DIM)),
        'cache_d_k': nrm((DEPTH, DEC_BATCH, PAST_LEN, N_HEADS, HEAD_DIM)),
        'cache_d_v': nrm((DEPTH, DEC_BATCH, PAST_LEN, N_HEADS, HEAD_DIM)),
        'cache_d_logf': jax.nn.log_sigmoid(FORGET_BIAS + nrm((DEPTH, DEC_BATCH, PAST_LEN, N_HEADS))),
        'p_prompt': nrm((DEPTH, BATCH, SEQ, PLE_DIM)),
        'p_sample': nrm((DEPTH, DEC_BATCH, DEC_SEQ, PLE_DIM)),
        'g_in': 1.0 + nrm((DEPTH, D_MODEL), 0.1),
        'w_in': nrm((DEPTH, D_MODEL, IN_WIDTH), D_MODEL ** -0.5),
        'g_qk': 1.0 + nrm((DEPTH, N_QK_GAINS, HEAD_DIM), 0.1),
        'g_rope': 1.0 + nrm((DEPTH, 2, MLA_ROPE), 0.1),
        'a_rel_bias': nrm((DEPTH, N_HEADS, 2 * REL_CLIP + 1), 0.2),
        'b_g_cq': 1.0 + nrm((DEPTH, MLA_Q_LORA), 0.1),
        'b_w_uq': nrm((DEPTH, MLA_Q_LORA, N_HEADS * (MLA_NOPE + MLA_ROPE)), MLA_Q_LORA ** -0.5),
        'b_g_ckv': 1.0 + nrm((DEPTH, MLA_KV_LORA), 0.1),
        'b_w_ukv': nrm((DEPTH, MLA_KV_LORA, N_HEADS * (MLA_NOPE + MLA_V)), MLA_KV_LORA ** -0.5),
        'd_b_f': FORGET_BIAS + nrm((DEPTH, N_HEADS), 0.5),
        'w_out': nrm((DEPTH, MIX_WIDTH, D_MODEL), MIX_WIDTH ** -0.5),
        'g_ple': 1.0 + nrm((DEPTH, D_MODEL), 0.1),
        'w_ple_gate': nrm((DEPTH, D_MODEL, D_MODEL), D_MODEL ** -0.5),
        'w_ple_proj': nrm((DEPTH, PLE_DIM, D_MODEL), PLE_DIM ** -0.5),
    }

def reference(x_prompt, x_sample, cache_a_k, cache_a_v, cache_b_ckv, cache_b_krope, cache_c_k, cache_c_v,
              cache_c_idx_k, cache_d_k, cache_d_v, cache_d_logf, p_prompt, p_sample, g_in, w_in, g_qk, g_rope,
              a_rel_bias, b_g_cq, b_w_uq, b_g_ckv, b_w_ukv, d_b_f, w_out, g_ple, w_ple_gate, w_ple_proj):
    B, T = x_prompt.shape[:2]
    dt = x_prompt.dtype
    fresh = (
        jnp.zeros((B, 0, N_HEADS, HEAD_DIM), dt), jnp.zeros((B, 0, N_HEADS, HEAD_DIM), dt),
        jnp.zeros((B, 0, MLA_KV_LORA), dt), jnp.zeros((B, 0, MLA_ROPE), dt),
        jnp.zeros((B, 0, HEAD_DIM), dt), jnp.zeros((B, 0, HEAD_DIM), dt), jnp.zeros((B, 0, IDX_DIM), dt),
        jnp.zeros((B, 0, N_HEADS, HEAD_DIM), dt), jnp.zeros((B, 0, N_HEADS, HEAD_DIM), dt),
        jnp.zeros((B, 0, N_HEADS), jnp.float32),
    )
    xp, xs = x_prompt, x_sample
    states_p, states_s = [], []
    for i in range(DEPTH):
        w = {
            'g_in': g_in[i], 'w_in': w_in[i], 'g_qk': g_qk[i], 'g_rope': g_rope[i], 'a_rel_bias': a_rel_bias[i],
            'b_g_cq': b_g_cq[i], 'b_w_uq': b_w_uq[i], 'b_g_ckv': b_g_ckv[i], 'b_w_ukv': b_w_ukv[i],
            'd_b_f': d_b_f[i], 'w_out': w_out[i], 'g_ple': g_ple[i], 'w_ple_gate': w_ple_gate[i],
            'w_ple_proj': w_ple_proj[i],
        }
        xp, st_p = trunk_layer(xp, p_prompt[i], fresh, w)
        past = (cache_a_k[i], cache_a_v[i], cache_b_ckv[i], cache_b_krope[i], cache_c_k[i], cache_c_v[i],
                cache_c_idx_k[i], cache_d_k[i], cache_d_v[i], cache_d_logf[i])
        xs, st_s = trunk_layer(xs, p_sample[i], past, w)
        states_p.append(st_p)
        states_s.append(st_s)
    (a_k_p, a_v_p, b_ckv_p, b_krope_p, c_k_p, c_v_p, c_idx_k_p, d_k_p, d_v_p, d_logf_p) = [jnp.stack(t) for t in zip(*states_p)]
    (a_k_s, a_v_s, b_ckv_s, b_krope_s, c_k_s, c_v_s, c_idx_k_s, d_k_s, d_v_s, d_logf_s) = [jnp.stack(t) for t in zip(*states_s)]
    keep = min(A_BAND, T)
    return (xp, xs,
            a_k_p[:, :, T - keep:], a_v_p[:, :, T - keep:], b_ckv_p, b_krope_p, c_k_p, c_v_p, c_idx_k_p, d_k_p, d_v_p, d_logf_p,
            a_k_s, a_v_s, b_ckv_s, b_krope_s, c_k_s, c_v_s, c_idx_k_s, d_k_s, d_v_s, d_logf_s)


_drawn_inputs = setup_inputs


def setup_inputs(seed=0):
    import zlib

    import numpy as np

    out = dict(_drawn_inputs(seed))
    spreads = {}
    factors = {'cache_b_krope': 3.038, 'cache_d_logf': 4.502, 'a_rel_bias': 8.0, 'b_g_cq': 8.0}
    for name, (base, spread) in spreads.items():
        noise = np.random.default_rng([zlib.crc32(name.encode()), seed]).standard_normal(out[name].shape)
        drawn = base * np.exp(spread * noise) if base else spread * noise
        out[name] = jnp.asarray(drawn.astype(out[name].dtype))
    for name, factor in factors.items():
        out[name] = (out[name] * factor).astype(out[name].dtype)
    return out
```

```python
from contextlib import ExitStack

import concourse.bass as bass
from concourse import mybir

ALU = mybir.AluOpType
ACT = mybir.ActivationFunctionType
F32 = mybir.dt.float32
BF16 = mybir.dt.bfloat16
AX = mybir.AxisListType

P = 128
DM = 1024
KC = DM // P
DEPTH = 2
NT = 9
TP = 8
H, HD = 4, 64
GW = H * HD
NB, NQ, PAST = 8, 16, 256
KEYS8 = PAST + NQ
PACKS = NB // 2
A, B, C, D = range(4)
EPS = 1e-6
NEG = -1e30
TAKEN = -3e38
TOPK_P, TOPK_S = 256, KEYS8 // 4
MLA_SCALE = 96.0 ** -0.5
IH, ID = 8, 32
CQ, CKV, RR = 384, 128, 32
GROUP_COL = [0, 1024, 1824, 2760]
IN_WIDTH = 3788
PIECES = {A: [(0, 0, 512), (1, 0, 512)], B: [(0, 0, 512), (1, 0, 288)],
          C: [(0, 0, 512), (1, 0, 424)], D: [(0, 0, 512), (1, 0, 260), (1, 260, 256)]}
CHUNK_W = {g: [512, sum(n for c, _, n in PIECES[g] if c == 1)] for g in range(4)}
STEPS = [(g, t) for g in range(4) for t in range(NT)]
BAND = 640


def first_key_tile(g, t):
    return max(0, t - 4) if g == A else 0


def keys_of(g, t):
    return (t + 1 - first_key_tile(g, t)) * P


def unit(g, t, i=0):
    return (g * NT + t) * 4 + i


LAST_TURN = {A: "tqk", B: "tk", C: "tix", D: "tqk"}


def indexed(t):
    return keys_of(C, t) > TOPK_P


def index_no(t, i):
    return (t - 2) * IH + i


IDX8 = (TP - 2) * IH


def schedule():
    o = []

    def project(g, t, i):
        o.append(("proj", g, t, i))
        c, col, n = PIECES[g][i]
        if t == 8 and col + n == CHUNK_W[g][c] and 2 * g + c + 3 < 8:
            o.append(("load_w", 2 * g + c + 3))

    def norms(g, t, part):
        if (part == 0) != (g == B):
            if g != B:
                o.append(("nsum", g, t))
            o.append(("rstd", g, t))
        if part == 1:
            o.append(("nmul", g, t))
            if g in (B, C):
                o.append(("rope", g, t))

    def latents(g, t):
        if g == B:
            o.extend([("tlat", t), ("upq", t), ("upk", t)])

    def late(g, t):
        if g == B:
            o.extend([("nsum2", t), ("rstd2", t), ("nmul2", t), ("rope2", t)])
        if g == D:
            o.append(("forget", t))
            if t < 8:
                o.append(("widen", t))

    def finish(g, t):
        o.append(("gate", g, t))
        o.extend({A: [("tqk", g, t)], B: [("tq", g, t), ("tk", g, t)], C: [("tqk", g, t), ("tix", g, t)],
                  D: [("tqk", g, t), ("tcum", t)]}[g])
        o.append(("states", g, t))

    for i in range(len(PIECES[A])):
        project(A, 0, i)
    norms(A, 0, 0)
    norms(A, 0, 1)
    finish(A, 0)
    for n, (g, t) in enumerate(STEPS):
        nx = STEPS[n + 1] if n + 1 < len(STEPS) else None
        pieces = len(PIECES[nx[0]]) if nx else 0

        def softmax(h):
            o.extend([("sc", g, t, h), ("sm", g, t, h)])
        if t < 8:
            if g == C:
                if indexed(t):
                    o.extend(("isc", t, i) for i in range(IH))
                o.append(("select", t))
            softmax(0)
            softmax(1)
            project(*nx, 0)
            o.append(("tp", g, t, 0))
            softmax(2)
            o.append(("pv", g, t, 0))
            norms(*nx, 0)
            project(*nx, 1)
            o.append(("tp", g, t, 1))
            softmax(3)
            o.append(("pv", g, t, 1))
            norms(*nx, 1)
            o.append(("tp", g, t, 2))
            if pieces > 2:
                project(*nx, 2)
            o.append(("pv", g, t, 2))
            latents(*nx)
            o.append(("tp", g, t, 3))
            o.append(("pv", g, t, 3))
            late(*nx)
            o.append(("y", g, t))
        else:
            o.append(("side", g))
            for p in range(PACKS):
                o.extend([("load_pack", g, p), ("q_diag", g, p)])
                if g == B:
                    for b2 in range(2):
                        for blk in range(2):
                            o.extend([("pj_past", p, b2, blk), ("t_past", p, b2, blk)])
                if g == C:
                    o.extend([("iq_diag", p), ("isc8", p, 0), ("isc8", p, 1), ("score8", p), ("select8", p)])
                o.append(("sc8", g, p))
                if p < pieces:
                    project(*nx, p)
                o.extend([("sm8", g, p), ("tp8", g, p)])
                if nx and p < 2:
                    norms(*nx, p)
                o.append(("pv8", g, p))
            o.append(("y8", g, t))
            if nx:
                latents(*nx)
                late(*nx)
        if nx:
            finish(*nx)
    return o


def count_uses(order):
    ordinal, kinds, pj, tb, ob = {}, {}, {}, {}, {}
    for key in order:
        st = key[0]
        kinds[st] = kinds.get(st, 0) + 1
        ordinal[key] = kinds[st]
        if st in ("proj", "upq", "upk", "pj_past"):
            pj[key] = len(pj) + 1
        if st in ("tlat", "tqk", "tix", "tq", "tk", "tcum", "tp8", "t_past", "y8"):
            tb[key] = len(tb) + 1
        if st == "tp":
            for j in range(-(-keys_of(key[1], key[2]) // 512)):
                tb[key + (j,)] = len(tb) + 1
        if st in ("score8", "pv8"):
            ob[key] = len(ob) + 1
        if st == "pv" and key[3] == 0:
            ob[key[:3]] = len(ob) + 1
    return ordinal, pj, tb, ob


def count_dmas():
    past, states, n, m = {}, {}, 0, 0
    for g in range(4):
        for p in range(PACKS):
            n += {A: 8, B: 7, C: 18, D: 24}[g]
            past[g, p] = n
        for t in range(NT):
            m += {A: 2 if t >= 4 else 0, B: 2, C: 3, D: 3}[g]
            states[g, t] = m
    return past, states


def build(nc, ins, outs, scratch):
    with ExitStack() as ctx:
        def sb(name, shape, dt=F32):
            return ctx.enter_context(nc.sbuf_tensor(name, shape, dt))

        def ps(name, shape, dt=F32):
            return ctx.enter_context(nc.psum_tensor(name, shape, dt))

        all_sems = []

        def sem(name):
            s = ctx.enter_context(nc.semaphore(name))
            all_sems.append(s)
            return s

        ident = sb("ident", [P, P])
        ident_h = sb("ident_h", [P, P], BF16)
        tri = sb("tri", [P, P])
        mask_chunk = sb("mask_chunk", [P, P], BF16)
        mask_causal = sb("mask_causal", [P, P], BF16)
        mask_new = sb("mask_new", [P, NQ])
        pick = sb("pick", [P, 64])
        rope_b = sb("rope_b", [P, 2, NT, 32])
        rope_c = sb("rope_c", [P, 2, NT, 16])
        half = sb("half", [P, 16])
        g_in_c = sb("g_in_c", [P, KC])
        g_ple_c = sb("g_ple_c", [P, KC])
        g_cq_c = sb("g_cq_c", [P, 3])
        gains = sb("gains", [P, 8, HD])
        g_ckv = sb("g_ckv", [P, CKV])
        g_rope = sb("g_rope", [P, 2, RR])
        b_f = sb("b_f", [P, H])
        w_uq = sb("w_uq", [P, 3, 384])
        w_ukv = sb("w_ukv", [P, 512])
        xn_t = sb("xn_t", [P, KC, NT * P])
        w_buf = sb("w_buf", [P, 3, KC * 516])
        ct = sb("ct", [P, H * 1024])
        bias_s = sb("bias_s", [P, KEYS8])
        nf = ct[:, :].rearrange("p (h n) -> p h n", h=H)
        band = ct[:, 0:H * BAND].rearrange("p (h n) -> p h n", h=H)

        def chunk_view(ci):
            return w_buf[:, ci % 3, 0:KC * CHUNK_W[ci // 2][ci % 2]].rearrange("p (c n) -> p c n", c=KC)

        def load_chunk(sp, l, ci):
            col = GROUP_COL[ci // 2] + 512 * (ci % 2)
            w = CHUNK_W[ci // 2][ci % 2]
            return sp.dma_start(chunk_view(ci),
                                lay(ins["w_in"], l)[:, col:col + w].rearrange("(c p) n -> p c n", p=P))

        pj = ps("pj", [P, 512])
        tb = ps("tb", [P, 2, 512])
        ob = ps("ob", [P, 512])
        sc = ps("sc", [P, 2, 1024])

        xs, mixd = scratch["xs"], scratch["mix"]

        def lay(ap, l):
            dims = " ".join(f"d{i}" for i in range(1, ap.ndim))
            names = dims.split()
            if len(names) == 1:
                return ap[bass.ds(l, 1), :].rearrange("a b -> (a b)")
            idx = (bass.ds(l, 1),) + (slice(None),) * (ap.ndim - 1)
            return ap[idx].rearrange(f"a {dims} -> (a {names[0]}) {' '.join(names[1:])}")

        s_load = sem("const_loaded")
        s_copy = sem("x_copied")
        s_id = sem("ident_built")

        with nc.Block() as block:
            @block.sync
            def _(sp):
                sp.dma_start(xs[0], ins["x0"]).then_inc(s_copy, 16)
                for dst, src in ((tri, "tri"), (mask_new, "mask_new"), (pick, "pick")):
                    sp.dma_start(dst[:, :], ins[src]).then_inc(s_load, 16)
                sp.dma_start(rope_b[:, :, :, :], ins["rope_b"]).then_inc(s_load, 16)
                sp.dma_start(rope_c[:, :, :, :], ins["rope_c"]).then_inc(s_load, 16)
                sp.wait_ge(s_load, 5 * 16)
                sp.wait_ge(s_copy, 16)

            @block.gpsimd
            def _(pool):
                counts = {}

                def own(s):
                    counts[s.name] = counts.get(s.name, 0) + 1
                    pool.wait_ge(s, counts[s.name])

                pool.memset(half[:, :], -0.5).then_inc(s_id, 1)
                own(s_id)
                pool.memset(ident[:, :], 0.0).then_inc(s_id, 1)
                own(s_id)
                pool.memset(ident_h[:, :], 0.0).then_inc(s_id, 1)
                own(s_id)
                pool.memset(mask_chunk[:, :], 0.0).then_inc(s_id, 1)
                own(s_id)
                pool.memset(mask_causal[:, :], 0.0).then_inc(s_id, 1)
                own(s_id)
                pool.wait_ge(s_id, 5)
                for m in (ident, ident_h):
                    pool.affine_select(out=m[:, :], in_=m[:, :], compare_op=ALU.not_equal, fill=1.0, base=0,
                                       pattern=[[-1, P]], channel_multiplier=1).then_inc(s_id, 1)
                    own(s_id)
                pool.affine_select(out=mask_causal[:, :], in_=mask_causal[:, :], compare_op=ALU.is_ge, fill=NEG,
                                   base=0, pattern=[[-1, P]], channel_multiplier=1).then_inc(s_id, 1)
                own(s_id)
                pool.memset(mask_chunk[0:64, 64:128], NEG).then_inc(s_id, 1)
                own(s_id)
                pool.wait_ge(s_id, 9)

        def clear_sems():
            for s in all_sems:
                nc.gpsimd.sem_clear(s)
            nc.all_engine_barrier()

        clear_sems()

        vec_loaded = sem("vec_loaded")
        w_first = sem("w_first")
        band_masked = sem("band_masked")
        x_loaded = [sem("x_loaded0"), sem("x_loaded1")]
        x_squared = sem("x_squared")
        x_rstd = sem("x_rstd")
        x_normed = sem("x_normed")
        gains_scaled = sem("gains_scaled")
        dve_step, act_step, pool_step = sem("dve_step"), sem("act_step"), sem("pool_step")
        w_loaded = [sem(f"w_loaded{i}") for i in range(3)]
        pj_full, pj_free = sem("pj_full"), sem("pj_free")
        t_full, t_free = sem("t_full"), sem("t_free")
        o_full, o_free = sem("o_full"), sem("o_free")
        s_full = sem("s_full")
        row_max = sem("row_max")
        probs_ready = sem("probs_ready")
        probs_scaled = sem("probs_scaled")
        pv_done = sem("pv_done")
        idx_full, idx_relu, idx_added = sem("idx_full"), sem("idx_relu"), sem("idx_added")
        stats_in, rstd_out = sem("stats_in"), sem("rstd_out")
        stats2_in, rstd2_out = sem("stats2_in"), sem("rstd2_out")
        statsp_in, rstdp_out, past_normed = sem("statsp_in"), sem("rstdp_out"), sem("past_normed")
        qk_ready, roped, normed2, roped2 = sem("qk_ready"), sem("roped"), sem("normed2"), sem("roped2")
        gated, mixed, mix_stored, state_stored = sem("gated"), sem("mixed"), sem("mix_stored"), sem("state_stored")
        forget_in, forget_ln, forget_out = sem("forget_in"), sem("forget_ln"), sem("forget_out")
        forget_wide = sem("forget_wide")
        past_loaded, side_written, side_loaded = sem("past_loaded"), sem("side_written"), sem("side_loaded")
        q_diag_ready, iq_diag_ready, wsel_ready = (sem("q_diag_ready"),
                                                           sem("iq_diag_ready"), sem("wsel_ready"))
        ot_ready = sem("ot_ready")
        out_w, mix_in, x_in, p_in = sem("out_w"), sem("mix_in"), sem("x_in"), sem("p_in")
        a_full, b_full, c_full = sem("out_full"), sem("gate_full"), sem("ple_full")
        x1_ready, sg_exp, x2_ready, x2_stored = sem("x1_ready"), sem("sg_exp"), sem("x2_ready"), sem("x2_stored")
        xn_ready = sem("xn_ready")

        order = schedule()
        ordinal, pj_use, t_use, o_use = count_uses(order)
        past_dmas, n_states = count_dmas()

        with nc.Fori(0, DEPTH) as layer:
            with ExitStack() as mem, nc.Block() as block:
                def s1(name, shape, dt=F32):
                    return mem.enter_context(nc.sbuf_tensor(name, shape, dt))
                xt = s1("xt", [P, 2, DM])
                xn = s1("xn", [P, 2, DM])
                sqj = s1("sqj", [P, DM])
                st1 = s1("st1", [P, 2 * NT])

                @block.sync
                def _(sp):
                    for t in range(NT):
                        if t >= 2:
                            sp.wait_ge(x_normed, t - 1)
                        sp.dma_start(xt[:, t % 2, :], lay(xs, layer)[t]).then_inc(x_loaded[t % 2], 16)
                        if t == 0:
                            for dst, src in ((g_in_c, "g_in"), (g_ple_c, "g_ple"), (g_cq_c, "g_cq")):
                                sp.dma_start(dst[:, :], lay(ins[src], layer)).then_inc(vec_loaded, 16)
                            sp.dma_start(gains[:, :, :], lay(ins["g_qk"], layer).unsqueeze(0)
                                         .to_broadcast([P, 8, HD])).then_inc(vec_loaded, 16)
                            sp.dma_start(g_ckv[:, :], ins["g_ckv"][bass.ds(layer, 1), :]
                                         .to_broadcast([P, CKV])).then_inc(vec_loaded, 16)
                            sp.dma_start(g_rope[:, :, :], lay(ins["g_rope"], layer).unsqueeze(0)
                                         .to_broadcast([P, 2, RR])).then_inc(vec_loaded, 16)
                            sp.dma_start(b_f[:, :], ins["b_f"][bass.ds(layer, 1), :]
                                         .to_broadcast([P, H])).then_inc(vec_loaded, 16)
                    for c in range(3):
                        load_chunk(sp, layer, c).then_inc(w_first, 16)
                    sp.dma_start(w_uq[:, :, :], lay(ins["w_uq"], layer).rearrange("(c p) n -> p c n", p=P)
                                 ).then_inc(w_first, 16)
                    sp.dma_start(w_ukv[:, :], lay(ins["w_ukv"], layer)).then_inc(w_first, 16)
                    sp.dma_start(band, lay(ins["bias_p"], layer)).then_inc(w_first, 16)
                    sp.dma_start(bias_s[:, :], lay(ins["bias_s"], layer)).then_inc(w_first, 16)
                    sp.wait_ge(w_first, 7 * 16)
                    sp.wait_ge(vec_loaded, 7 * 16)

                @block.gpsimd
                def _(pool):
                    counts = {}

                    def own(s):
                        counts[s.name] = counts.get(s.name, 0) + 1
                        pool.wait_ge(s, counts[s.name])

                    for t in range(NT):
                        pool.wait_ge(x_squared, t + 1)
                        pool.tensor_scalar(st1[:, NT + t:NT + t + 1], st1[:, t:t + 1], EPS, None,
                                           ALU.add).then_inc(pool_step, 1)
                        own(pool_step)
                        pool.wait_ge(pool_step, t + 1)
                        pool.tensor_tensor(st1[:, NT + t:NT + t + 1], st1[:, NT + t:NT + t + 1],
                                           half[:, 0:1], ALU.pow).then_inc(x_rstd, 1)
                        own(x_rstd)
                    pool.wait_ge(w_first, 7 * 16)
                    pool.memset(band[0:64, :, BAND - 64:BAND], NEG).then_inc(band_masked, 1)
                    own(band_masked)
                    pool.memset(band[64:128, :, 0:64], NEG).then_inc(band_masked, 1)
                    own(band_masked)
                    pool.wait_ge(band_masked, 2)

                @block.scalar
                def _(act):
                    counts = {}

                    def own(s):
                        counts[s.name] = counts.get(s.name, 0) + 1
                        act.wait_ge(s, counts[s.name])

                    def square(t):
                        act.wait_ge(x_loaded[t % 2], 16 * (t // 2 + 1))
                        if t:
                            act.wait_ge(x_squared, t)
                        act.activation(sqj[:, :], xt[:, t % 2, :], ACT.Square, scale=DM ** -0.5,
                                       accum_out=st1[:, t:t + 1]).then_inc(x_squared, 1)
                        own(x_squared)
                    square(0)
                    for t in range(NT):
                        if t + 1 < NT:
                            square(t + 1)
                        if t == 0:
                            act.wait_ge(vec_loaded, 7 * 16)
                        for j in range(2):
                            act.wait_ge(t_full, 2 * t + j + 1)
                            for k in range(4):
                                a = act.activation(xn_t[:, 4 * j + k, t * P:(t + 1) * P],
                                                   tb[:, j, k * P:(k + 1) * P], ACT.Copy,
                                                   scale=g_in_c[:, 4 * j + k:4 * j + k + 1])
                            a.then_inc(t_free, 1)
                            own(t_free)

                @block.vector
                def _(dve):
                    counts = {}

                    def own(s):
                        counts[s.name] = counts.get(s.name, 0) + 1
                        dve.wait_ge(s, counts[s.name])

                    dve.wait_ge(vec_loaded, 7 * 16)
                    for i in (0, 2, 4):
                        dve.tensor_scalar(gains[:, i, :], gains[:, i, :], HD ** -0.5, None,
                                          ALU.mult).then_inc(gains_scaled, 1)
                        own(gains_scaled)
                    for t in range(NT):
                        dve.wait_ge(x_rstd, t + 1)
                        if t >= 2:
                            dve.wait_ge(t_full, 2 * (t - 1))
                        dve.tensor_scalar(xn[:, t % 2, :], xt[:, t % 2, :], st1[:, NT + t:NT + t + 1], None,
                                          ALU.mult).then_inc(x_normed, 1)
                        own(x_normed)

                @block.tensor
                def _(pe):
                    for t in range(NT):
                        pe.wait_ge(x_normed, t + 1)
                        for j in range(2):
                            if t:
                                pe.wait_ge(t_free, 2 * t + j - 1)
                            for k in range(4):
                                c = 4 * j + k
                                m = nc.tensor.transpose(tb[:, j, k * P:(k + 1) * P],
                                                        xn[:, t % 2, c * P:(c + 1) * P], ident[:, :])
                            m.then_inc(t_full, 1)
            clear_sems()

            with ExitStack() as mem, nc.Block() as block:
                def s2(name, shape, dt=F32):
                    return mem.enter_context(nc.sbuf_tensor(name, shape, dt))

                def kt_past(c):
                    return nf[:, c, 512:1024].rearrange("p (b n) -> p b n", b=2)

                def v_past(b2, blk):
                    return nf[:, 2 * b2 + blk, 256:512]

                kt = s2("kt", [P, 4, 1024])
                vv = s2("vv", [P, TP, GW])
                kt8 = s2("kt8", [P, 3, P])
                v8 = s2("v8", [P, GW])
                qt = s2("qt", [P, 2, 4, P])
                z = s2("z", [P, 1028])
                sq = s2("sq", [P, 512])
                sq2 = s2("sq2", [P, GW])
                qk = s2("qk", [P, 512])
                bq = s2("bq", [P, H, 96])
                bk = s2("bk", [P, H, 96])
                eg = s2("eg", [P, GW])
                gate = s2("gate", [P, 2, GW])
                mixt = s2("mixt", [P, 2, GW])
                probs = s2("probs", [P, 2, 1024])
                pt = s2("pt", [P, 2, 1024])
                lat_t = s2("lat_t", [P, 4, P])
                kr = s2("kr", [P, 2, RR])
                acc = s2("acc", [P, 1024])
                iqt = s2("iqt", [P, 2, 2, P])
                iw = s2("iw", [P, 2, IH])
                ik4 = s2("ik4", [P, 4, ID])
                top8 = s2("top8", [P, 8])
                iq_diag = s2("iq_diag", [P, 2, 2, P])
                ik_past = s2("ik_past", [P, 2, PAST])
                ckv_past = ik_past
                iw_rows = s2("iw_rows", [P, NB])
                wsel = s2("wsel", [P, 2, 64])
                q_diag = s2("q_diag", [P, 2, 3, 2, 64])
                v_new = s2("v_new", [NQ, 2, GW])
                kp = s2("kp", [P, GW])
                y8 = kp
                ot8 = s2("ot8", [P, 2, P])
                fl = s2("fl", [P, 7, H])
                lfw = s2("lfw", [P, H, P])
                nlf_row = s2("nlf_row", [P, KEYS8])
                nf8 = nlf_row
                zero_row = lfw[:, :, :].rearrange("p h n -> p (h n)")[:, 0:KEYS8]
                lf_t = s2("lf_t", [H, P])
                stats = s2("stats", [P, 24])
                rstd = s2("rstd", [P, 24])
                mx = s2("mx", [P, 2])
                nmx = s2("nmx", [P, 2])
                sm = s2("sm", [P, 4])
                rs = s2("rs", [P, 4])
                rt = s2("rt", [P, 2, 5 * 32])

                def v_dst(t):
                    return v8[:, :] if t == 8 else vv[:, t, :]

                @block.sync
                def _(sp):
                    def states(g, t):
                        def put(name, src, row=t):
                            sp.dma_start(lay(outs[name], layer)[row], src).then_inc(state_stored, 16)
                        n = ordinal["nmul", g, t]
                        sp.wait_ge(qk_ready, n)
                        if g in (B, C):
                            sp.wait_ge(roped, ordinal["rope", g, t])
                        sp.wait_ge(pj_free, pj_use["proj", g, t, len(PIECES[g]) - 1])
                        if g == A and t >= 4:
                            put("a_k", qk[:, 256:512], t - 4)
                            put("a_v", v_dst(t), t - 4)
                        if g == B:
                            put("b_ckv", qk[:, 384:512])
                            put("b_kr", kr[:, 1, :])
                        if g == C:
                            put("c_k", qk[:, 256:320])
                            put("c_v", z[:, 320:384])
                            put("c_ik", z[:, 640:672])
                        if g == D:
                            put("d_k", qk[:, 256:512])
                            put("d_v", v_dst(t))
                            sp.wait_ge(forget_out, t + 1)
                            put("d_lf", fl[:, 5, :])

                    def side(g):
                        if g == C:
                            sp.wait_ge(roped, ordinal["rope", C, 8])
                            sp.dma_start(scratch["iw"], iw[:, 0, :]).then_inc(side_written, 16)
                            sp.wait_ge(side_written, 16)
                            for ih in range(IH):
                                sp.dma_start(iw_rows[ih * NQ:(ih + 1) * NQ, :],
                                             scratch["iw"].rearrange("(b q) i -> i q b", q=NQ)[ih],
                                             allow_slow_non_contiguous=True).then_inc(side_loaded, 16)
                        if g == D:
                            sp.wait_ge(t_free, t_use["tcum", 8])
                            sp.dma_start(scratch["lf"], lf_t[:, :]).then_inc(side_written, 16)
                            sp.wait_ge(side_written, 32)

                    def load_pack(g, p):
                        def get(dst, src):
                            sp.dma_start(dst, src).then_inc(past_loaded, 16)
                        sp.wait_ge(pv_done, unit(g, 8, p))
                        sp.wait_ge(pj_free, pj_use["proj", g, 8, len(PIECES[g]) - 1])
                        if g == C:
                            sp.wait_ge(t_free, t_use["tix", C, 8])
                        two = [(b2, 2 * p + b2) for b2 in range(2)]
                        pack = slice(2 * p, 2 * p + 2)
                        if g in (A, D):
                            n = "a" if g == A else "d"
                            for c in range(2):
                                get(kt_past(c), lay(ins[n + "_kt"], layer)[c, :, pack, :])
                            for b2, b in two:
                                for blk in range(2):
                                    get(v_past(b2, blk), lay(ins[n + "_v"], layer)[b, blk * P:(blk + 1) * P, :])
                        if g == C:
                            for j in range(2):
                                get(kt_past(0)[64 * j:64 * j + 64], lay(ins["c_kt"], layer)[:, pack, :])
                                for b2, b in two:
                                    for blk in range(2):
                                        get(v_past(b2, blk)[:, 64 * j:64 * j + 64],
                                            lay(ins["c_v"], layer)[b, blk * P:(blk + 1) * P, :])
                            for j in range(4):
                                get(ik_past[32 * j:32 * j + 32], lay(ins["c_ikt"], layer)[:, pack, :])
                        if g == B:
                            get(ckv_past[:, :, :], lay(ins["b_ckvt"], layer)[:, pack, :])
                            for j in range(4):
                                get(kt_past(2)[32 * j:32 * j + 32], lay(ins["b_krt"], layer)[:, pack, :])
                        if g == D:
                            for b2, b in two:
                                for h in range(H):
                                    r = 64 * b2 + NQ * h
                                    get(nlf_row[r:r + NQ, 0:PAST],
                                        lay(ins["d_lft"], layer)[b, h:h + 1, :].to_broadcast([NQ, PAST]))
                                    get(nlf_row[r:r + NQ, PAST:KEYS8],
                                        scratch["lf"][h:h + 1, b * NQ:(b + 1) * NQ].to_broadcast([NQ, NQ]))
                        for b2, b in two:
                            for j in range(2 if g == C else 1):
                                w = 64 if g == C else GW
                                get(v_new[:, b2, w * j:w * (j + 1)], v8[b * NQ:(b + 1) * NQ, 0:w])

                    for st, *a in order:
                        if st == "states":
                            states(*a)
                        elif st == "side":
                            side(*a)
                        elif st == "load_pack":
                            load_pack(*a)
                        elif st == "load_w":
                            (ci,) = a
                            g, c = divmod(ci - 3, 2)
                            last = max(i for i, piece in enumerate(PIECES[g]) if piece[0] == c)
                            sp.wait_ge(pj_full, pj_use["proj", g, 8, last])
                            load_chunk(sp, layer, ci).then_inc(w_loaded[ci % 3], 16)
                        elif st in ("y", "y8"):
                            g, t = a
                            sp.wait_ge(mixed, g * NT + t + 1)
                            sp.dma_start(mixd[t, :, g * GW:(g + 1) * GW], mixt[:, t % 2, :]).then_inc(mix_stored, 16)
                    sp.wait_ge(mix_stored, 16 * len(STEPS))
                    sp.wait_ge(state_stored, 16 * n_states[D, 8])

                @block.tensor
                def _(pe):
                    def turn_bank(key):
                        n = t_use[key]
                        if n > 2:
                            pe.wait_ge(t_free, n - 2)
                        return tb[:, (n - 1) % 2, :]

                    def pj_bank(key):
                        if pj_use[key] > 1:
                            pe.wait_ge(pj_free, pj_use[key] - 1)

                    def o_bank(key):
                        if o_use[key] > 1:
                            pe.wait_ge(o_free, o_use[key] - 1)

                    def turn(b, srcs, rows=P):
                        for j, src in enumerate(srcs):
                            m = nc.tensor.transpose(b[0:rows, j * P:j * P + P], src, ident[:, :])
                        m.then_inc(t_full, 1)

                    def project(g, t, i):
                        c, col, n = PIECES[g][i]
                        ci = 2 * g + c
                        if ci >= 3 and t == 0 and col == 0:
                            pe.wait_ge(w_loaded[ci % 3], 16 * (ci // 3))
                        pj_bank(("proj", g, t, i))
                        w = chunk_view(ci)
                        for k in range(KC):
                            m = nc.tensor.matmul(pj[:, 0:n], xn_t[:, k, t * P:(t + 1) * P], w[:, k, col:col + n],
                                                 start=k == 0, stop=k == KC - 1)
                        m.then_inc(pj_full, 1)

                    def scores(g, t, h):
                        u = unit(g, t, h)
                        if u >= 2:
                            pe.wait_ge(row_max, u - 1)
                        if h == 0:
                            pe.wait_ge(t_free, t_use[LAST_TURN[g], g, t])
                        lo, n = first_key_tile(g, t) * P, keys_of(g, t)
                        for k0 in range(0, n, 512):
                            k1 = min(k0 + 512, n)
                            diag = g in (B, D) and k1 == n
                            if g == B:
                                l, r = qt[0:96, t % 2, h, :], kt[0:96, h, lo + k0:lo + k1]
                            else:
                                q0 = 64 * (h % 2)
                                l = qt[q0:q0 + 64, t % 2, h // 2, :]
                                r = kt[q0:q0 + 64, 0 if g == C else h // 2, lo + k0:lo + k1]
                            m = nc.tensor.matmul(sc[:, u % 2, k0:k1], l, r, start=True, stop=not diag)
                            if diag:
                                m = nc.tensor.matmul(sc[:, u % 2, n - P:n], ident_h[:, :],
                                                     (mask_chunk if g == B else mask_causal)[:, :],
                                                     start=False, stop=True)
                        m.then_inc(s_full, 1)

                    def turn_probs(g, t, h):
                        u = unit(g, t, h)
                        pe.wait_ge(probs_ready, u + 1)
                        nk = keys_of(g, t) // P
                        for j in range(-(-nk // 4)):
                            turn(turn_bank(("tp", g, t, h, j)),
                                 [probs[:, u % 2, k * P:(k + 1) * P] for k in range(4 * j, min(nk, 4 * j + 4))])

                    def values(g, t, h):
                        u = unit(g, t, h)
                        if h == 0:
                            o_bank(("pv", g, t))
                        lo, nk = first_key_tile(g, t), keys_of(g, t) // P
                        pe.wait_ge(t_free, t_use["tp", g, t, h, -(-nk // 4) - 1])
                        c0 = 0 if g == C else h * HD
                        for k in range(nk):
                            m = nc.tensor.matmul(ob[:, h * HD:(h + 1) * HD], pt[:, u % 2, k * P:(k + 1) * P],
                                                 vv[:, lo + k, c0:c0 + HD], start=k == 0, stop=k == nk - 1)
                        m.then_inc(pv_done, 1)

                    for st, *a in order:
                        if st == "proj":
                            g, t, i = a
                            project(g, t, i)
                        elif st == "tlat":
                            (t,) = a
                            pe.wait_ge(qk_ready, ordinal["nmul", B, t])
                            turn(turn_bank(("tlat", t)), [qk[:, j * P:(j + 1) * P] for j in range(4)])
                        elif st == "upq":
                            (t,) = a
                            pe.wait_ge(t_free, t_use["tlat", t])
                            pj_bank(("upq", t))
                            for j in range(3):
                                m = nc.tensor.matmul(pj[:, 0:384], lat_t[:, j, :], w_uq[:, j, :],
                                                     start=j == 0, stop=j == 2)
                            m.then_inc(pj_full, 1)
                        elif st == "upk":
                            (t,) = a
                            pj_bank(("upk", t))
                            nc.tensor.matmul(pj[:, :], lat_t[:, 3, :], w_ukv[:, :], start=True,
                                             stop=True).then_inc(pj_full, 1)
                        elif st == "tqk":
                            g, t = a
                            if g == C:
                                pe.wait_ge(roped, ordinal["rope", C, t])
                            else:
                                pe.wait_ge(qk_ready, ordinal["nmul", g, t])
                            turn(turn_bank(("tqk", g, t)), [qk[:, j * P:(j + 1) * P] for j in range(3 if g == C else 4)])
                        elif st == "tix":
                            g, t = a
                            turn(turn_bank(("tix", g, t)), [z[:, 384:512], z[:, 512:640],
                                                            ik4[:, :, :].rearrange("p a b -> p (a b)")])
                        elif st in ("tq", "tk"):
                            g, t = a
                            pe.wait_ge(roped2, t + 1)
                            src = bq if st == "tq" else bk
                            b = turn_bank((st, g, t))
                            if t < 8:
                                turn(b, [src[:, h, :] for h in range(H)], 96)
                            else:
                                c0 = 0 if st == "tq" else 384
                                turn(b, [z[:, c0 + j * P:c0 + (j + 1) * P] for j in range(3)])
                        elif st == "tcum":
                            (t,) = a
                            b = turn_bank(("tcum", t))
                            if t < 8:
                                pe.wait_ge(forget_wide, t + 1)
                                for h in range(H):
                                    m = nc.tensor.matmul(b[:, h * P:(h + 1) * P], lfw[:, h, :], tri[:, :],
                                                         start=True, stop=True)
                                m.then_inc(t_full, 1)
                            else:
                                pe.wait_ge(forget_out, t + 1)
                                nc.tensor.transpose(b[0:H, 0:P], fl[:, 6, :], ident[:, :]).then_inc(t_full, 1)
                        elif st == "isc":
                            t, i = a
                            x = index_no(t, i)
                            if i == 0:
                                pe.wait_ge(t_free, t_use["tix", C, t])
                                pe.wait_ge(row_max, unit(C, t))
                            if x >= 2:
                                pe.wait_ge(idx_relu, x - 1)
                            r = 32 * (i % 4)
                            for k0 in range(0, keys_of(C, t), 512):
                                k1 = min(k0 + 512, keys_of(C, t))
                                m = nc.tensor.matmul(sc[:, x % 2, k0:k1], iqt[r:r + 32, t % 2, i // 4, :],
                                                     kt[r:r + 32, 1, k0:k1], start=True, stop=True)
                            m.then_inc(idx_full, 1)
                            if i == IH - 1:
                                pe.wait_ge(idx_relu, x + 1)
                        elif st == "sc":
                            scores(*a)
                        elif st == "tp":
                            turn_probs(*a)
                        elif st == "pv":
                            values(*a)
                        elif st == "pj_past":
                            p, b2, blk = a
                            if (b2, blk) == (0, 0):
                                pe.wait_ge(past_loaded, 16 * past_dmas[B, p])
                            pj_bank(("pj_past", p, b2, blk))
                            nc.tensor.matmul(pj[:, :], ckv_past[:, b2, blk * P:(blk + 1) * P], w_ukv[:, :],
                                             start=True, stop=True).then_inc(pj_full, 1)
                        elif st == "t_past":
                            p, b2, blk = a
                            pe.wait_ge(past_normed, ordinal["t_past", p, b2, blk])
                            turn(turn_bank(("t_past", p, b2, blk)), [kp[:, 0:P], kp[:, P:2 * P]])
                        elif st == "isc8":
                            p, b2 = a
                            x = IDX8 + 2 * p + b2
                            if b2 == 0:
                                pe.wait_ge(row_max, unit(C, 8, p))
                                pe.wait_ge(past_loaded, 16 * past_dmas[C, p])
                                pe.wait_ge(iq_diag_ready, p + 1)
                                pe.wait_ge(t_free, t_use["tix", C, 8])
                            pe.wait_ge(idx_relu, x - 1)
                            new = slice((2 * p + b2) * NQ, (2 * p + b2 + 1) * NQ)
                            for k0, k1, r in ((0, PAST, ik_past[:, b2, :]), (PAST, KEYS8, kt8[:, 1, new])):
                                for c in range(2):
                                    m = nc.tensor.matmul(sc[:, x % 2, k0:k1], iq_diag[:, c, b2, :], r,
                                                         start=c == 0, stop=c == 1)
                            m.then_inc(idx_full, 1)
                        elif st == "score8":
                            (p,) = a
                            o_bank(("score8", p))
                            pe.wait_ge(wsel_ready, p + 1)
                            for b2 in range(2):
                                x = IDX8 + 2 * p + b2
                                pe.wait_ge(idx_relu, x + 1)
                                m = nc.tensor.matmul(ob[64 * b2:64 * b2 + 64, 0:KEYS8], wsel[:, b2, :],
                                                     probs[:, x % 2, 0:KEYS8], start=True, stop=True)
                            m.then_inc(o_full, 1)
                        elif st == "sc8":
                            g, p = a
                            u = unit(g, 8, p)
                            pe.wait_ge(row_max, u - 1)
                            pe.wait_ge(q_diag_ready, g * PACKS + p + 1)
                            pe.wait_ge(past_loaded, 16 * past_dmas[g, p])
                            if p == 0:
                                pe.wait_ge(t_free, t_use[LAST_TURN[g], g, 8])
                            if g == B:
                                pe.wait_ge(t_free, t_use["t_past", p, 1, 1])
                            for b2 in range(2):
                                new = slice((2 * p + b2) * NQ, (2 * p + b2 + 1) * NQ)
                                nchunk = 3 if g == B else 2
                                for k0, k1 in ((0, PAST), (PAST, KEYS8)):
                                    for c in range(nchunk):
                                        cc = 0 if g == C else c
                                        r = kt_past(cc)[:, b2, :] if k0 == 0 else kt8[:, cc, new]
                                        m = nc.tensor.matmul(sc[64 * b2:64 * b2 + 64, u % 2, k0:k1],
                                                             q_diag[:, p % 2, c, b2, :], r,
                                                             start=c == 0, stop=c == nchunk - 1)
                            m.then_inc(s_full, 1)
                        elif st == "tp8":
                            g, p = a
                            u = unit(g, 8, p)
                            pe.wait_ge(probs_scaled, g * PACKS + p + 1)
                            b = turn_bank(("tp8", g, p))
                            for k in range(3):
                                w = P if k < 2 else NQ
                                m = nc.tensor.transpose(b[0:w, k * P:(k + 1) * P],
                                                        probs[:, u % 2, k * P:k * P + w], ident[:, :])
                            m.then_inc(t_full, 1)
                        elif st == "pv8":
                            g, p = a
                            u = unit(g, 8, p)
                            o_bank(("pv8", g, p))
                            pe.wait_ge(t_free, t_use["tp8", g, p])
                            for b2 in range(2):
                                for hp in range(2):
                                    c0 = 0 if g == C else hp * P
                                    for k in range(3):
                                        w = P if k < 2 else NQ
                                        v = v_past(b2, k)[:, c0:c0 + P] if k < 2 else v_new[:, b2, c0:c0 + P]
                                        m = nc.tensor.matmul(ob[:, (2 * b2 + hp) * 64:(2 * b2 + hp + 1) * 64], v,
                                                             pt[0:w, u % 2, k * P + 64 * b2:k * P + 64 * b2 + 64],
                                                             start=k == 0, stop=k == 2)
                            m.then_inc(pv_done, 1)
                        elif st == "y8":
                            g, t = a
                            pe.wait_ge(ot_ready, (H - 1) * PACKS * (g + 1))
                            pe.wait_ge(o_free, o_use["pv8", g, PACKS - 1])
                            turn(turn_bank(("y8", g, t)), [ot8[:, 0, :], ot8[:, 1, :]])

                @block.scalar
                def _(act):
                    counts = {}

                    def own(s):
                        counts[s.name] = counts.get(s.name, 0) + 1
                        act.wait_ge(s, counts[s.name])

                    
                    def link(ins):
                        ins.then_inc(act_step, 1)
                        own(act_step)

                    def copy(dst, src, **kw):
                        return act.activation(dst, src, ACT.Copy, **kw)

                    def turned(key):
                        act.wait_ge(t_full, t_use[key])
                        return tb[:, (t_use[key] - 1) % 2, :]

                    def gate_exp(col):
                        copy(z[:, 768:1024], pj[:, col:col + GW])
                        act.activation(eg[:, :], pj[:, col:col + GW], ACT.Exp, scale=-1.0).then_inc(pj_free, 1)
                        own(pj_free)

                    def evac(g, t, i):
                        n = g * NT + t
                        act.wait_ge(pj_full, pj_use["proj", g, t, i])
                        if n and i == 0:
                            pg, ptile = STEPS[n - 1]
                            act.wait_ge(gated, n)
                            if pg in (B, C):
                                act.wait_ge(roped, ordinal["rope", pg, ptile])
                            act.wait_ge(state_stored, 16 * n_states[pg, ptile])
                            if t == 8 and g:
                                act.wait_ge(past_loaded, 16 * past_dmas[g - 1, PACKS - 1])
                        if i == 0:
                            copy(z[:, 0:512], pj[:, :])
                            if g == B:
                                act.activation(sq[:, 0:CQ], pj[:, 0:CQ], ACT.Square, scale=CQ ** -0.5,
                                               accum_out=stats[:, 0:1])
                                act.activation(sq[:, CQ:512], pj[:, CQ:512], ACT.Square, scale=CKV ** -0.5,
                                               accum_out=stats[:, 1:2]).then_inc(pj_free, 1)
                                own(pj_free)
                            else:
                                w = 320 if g == C else 512
                                if g == C:
                                    copy(v_dst(t)[:, 0:64], pj[:, 320:384])
                                act.activation(sq[:, 0:w], pj[:, 0:w], ACT.Square,
                                               scale=HD ** -0.5).then_inc(pj_free, 1)
                                own(pj_free)
                        elif g == A:
                            copy(v_dst(t), pj[:, 0:256])
                            gate_exp(256)
                        elif g == B:
                            copy(z[:, 512:544], pj[:, 0:32])
                            act.activation(sq2[:, 0:32], pj[:, 0:32], ACT.Square, scale=RR ** -0.5,
                                           accum_out=stats[:, 2:3])
                            gate_exp(32)
                        elif g == C:
                            copy(z[:, 512:680], pj[:, 0:168])
                            gate_exp(168)
                        elif i == 1:
                            copy(v_dst(t), pj[:, 0:256])
                            copy(z[:, 512:516], pj[:, 256:260]).then_inc(pj_free, 1)
                            own(pj_free)
                        else:
                            gate_exp(0)

                    def heads(x, n=H):
                        return x.rearrange("p (h n) -> p h n", h=n)

                    for st, *a in order:
                        if st == "proj":
                            evac(*a)
                        elif st == "tlat":
                            b = turned(("tlat", *a))
                            for j in range(3):
                                copy(lat_t[:, j, :], b[:, j * P:(j + 1) * P], scale=g_cq_c[:, j:j + 1])
                            copy(lat_t[:, 3, :], b[:, 3 * P:4 * P]).then_inc(t_free, 1)
                            own(t_free)
                        elif st == "upq":
                            act.wait_ge(pj_full, pj_use["upq", a[0]])
                            pv, sv = heads(pj[:, 0:384]), heads(sq[:, 0:384])
                            copy(bq[:, :, :], pv)
                            act.activation(sv[:, :, 0:64], pv[:, :, 0:64], ACT.Square, scale=HD ** -0.5)
                            act.activation(sv[:, :, 64:96], pv[:, :, 64:96], ACT.Square,
                                           scale=RR ** -0.5).then_inc(pj_free, 1)
                            own(pj_free)
                        elif st == "upk":
                            (t,) = a
                            act.wait_ge(pj_full, pj_use["upk", t])
                            pv = heads(pj[:, :])
                            copy(bk[:, :, 0:64], pv[:, :, 0:64])
                            copy(heads(v_dst(t)), pv[:, :, 64:128])
                            act.activation(heads(sq2[:, :]), pv[:, :, 0:64], ACT.Square,
                                           scale=HD ** -0.5).then_inc(pj_free, 1)
                            own(pj_free)
                        elif st in ("tq", "tk"):
                            g, t = a
                            b = turned((st, g, t))
                            if t < 8:
                                dst = qt[0:96, t % 2, :, :] if st == "tq" else kt[0:96, :, t * P:(t + 1) * P]
                                copy(dst, heads(b[0:96, :])).then_inc(t_free, 1)
                                own(t_free)
                            else:
                                copy(qt[:, 0, 0:3, :] if st == "tq" else kt8[:, :, :],
                                     heads(b[:, 0:3 * P], 3)).then_inc(t_free, 1)
                                own(t_free)
                        elif st == "tqk":
                            g, t = a
                            b = heads(turned((st, g, t)))
                            copy(qt[:, t % 2, 0:2, :], b[:, 0:2, :])
                            nk = 1 if g == C else 2
                            copy(kt8[:, 0:nk, :] if t == 8 else kt[:, 0:nk, t * P:(t + 1) * P],
                                 b[:, 2:2 + nk, :]).then_inc(t_free, 1)
                            own(t_free)
                        elif st == "tix":
                            g, t = a
                            b = heads(turned((st, g, t)))
                            copy(iqt[:, t % 2, :, :], b[:, 0:2, :])
                            copy(kt8[:, 1, :] if t == 8 else kt[:, 1, t * P:(t + 1) * P],
                                 b[:, 2, :]).then_inc(t_free, 1)
                            own(t_free)
                        elif st == "forget":
                            (t,) = a
                            act.wait_ge(forget_in, t + 1)
                            link(act.activation(fl[:, 2, :], fl[:, 1, :], ACT.Exp, scale=-1.0))
                            act.activation(fl[:, 3, :], fl[:, 2, :], ACT.Ln, bias=1.0).then_inc(forget_ln, 1)
                            own(forget_ln)
                        elif st == "tcum":
                            (t,) = a
                            b = turned(("tcum", t))
                            if t == 8:
                                copy(lf_t[:, :], b[0:H, 0:P]).then_inc(t_free, 1)
                                own(t_free)
                            else:
                                if t:
                                    act.wait_ge(t_free, t_use["tcum", t - 1])
                                for h in range(H):
                                    dst = nf[:, h, t * P:(t + 1) * P]
                                    if t == 0:
                                        x = copy(dst, b[:, h * P:(h + 1) * P])
                                    else:
                                        x = act.activation(dst, b[:, h * P:(h + 1) * P], ACT.Identity,
                                                           bias=nf[:, h, t * P - 1:t * P])
                                x.then_inc(t_free, 1)
                                own(t_free)
                        elif st in ("isc", "isc8"):
                            if st == "isc":
                                x, n = index_no(*a), keys_of(C, a[0])
                            else:
                                x, n = IDX8 + 2 * a[0] + a[1], KEYS8
                            act.wait_ge(idx_full, x + 1)
                            if x >= 2:
                                if st == "isc":
                                    act.wait_ge(idx_added, x - 1)
                                elif a[0] == 0:
                                    act.wait_ge(idx_added, IDX8)
                            act.activation(probs[:, x % 2, 0:n], sc[:, x % 2, 0:n], ACT.Relu,
                                           scale=ID ** -0.5).then_inc(idx_relu, 1)
                            own(idx_relu)
                        elif st in ("sm", "sm8"):
                            g, t, h = a if st == "sm" else (a[0], 8, a[1])
                            u = unit(g, t, h)
                            n = keys_of(g, t) if t < 8 else KEYS8
                            act.wait_ge(row_max, u + 1)
                            act.activation(probs[:, u % 2, 0:n], probs[:, u % 2, 0:n], ACT.Exp,
                                           bias=nmx[:, u % 2:u % 2 + 1],
                                           accum_out=sm[:, u % 4:u % 4 + 1]).then_inc(probs_ready, 1)
                            own(probs_ready)
                        elif st == "tp":
                            g, t, h = a
                            u = unit(g, t, h)
                            nk = keys_of(g, t) // P
                            for j in range(-(-nk // 4)):
                                w = min(nk - 4 * j, 4) * P
                                b = turned(("tp", g, t, h, j))
                                copy(pt[:, u % 2, 512 * j:512 * j + w], b[:, 0:w]).then_inc(t_free, 1)
                                own(t_free)
                        elif st == "tp8":
                            g, p = a
                            u = unit(g, 8, p)
                            b = turned(("tp8", g, p))
                            copy(pt[:, u % 2, 0:2 * P], b[:, 0:2 * P])
                            copy(pt[0:NQ, u % 2, 2 * P:3 * P], b[0:NQ, 2 * P:3 * P]).then_inc(t_free, 1)
                            own(t_free)
                        elif st == "pj_past":
                            p, b2, blk = a
                            act.wait_ge(pj_full, pj_use["pj_past", p, b2, blk])
                            pv = heads(pj[:, :])
                            copy(heads(kp[:, :]), pv[:, :, 0:64])
                            copy(heads(v_past(b2, blk)), pv[:, :, 64:128])
                            act.activation(heads(sq2[:, :]), pv[:, :, 0:64], ACT.Square,
                                           scale=HD ** -0.5).then_inc(pj_free, 1)
                            own(pj_free)
                        elif st == "t_past":
                            p, b2, blk = a
                            b = turned((st, *a))
                            for c in range(2):
                                x = copy(kt_past(c)[:, b2, blk * P:(blk + 1) * P], b[:, c * P:(c + 1) * P])
                            x.then_inc(t_free, 1)
                            own(t_free)
                        elif st == "y8":
                            copy(y8[:, :], turned((st, *a))[:, 0:2 * P]).then_inc(t_free, 1)
                            own(t_free)

                @block.vector
                def _(dve):
                    counts = {}

                    def own(s):
                        counts[s.name] = counts.get(s.name, 0) + 1
                        dve.wait_ge(s, counts[s.name])

                    
                    def link(ins):
                        ins.then_inc(dve_step, 1)
                        own(dve_step)

                    def heads(x, n=H):
                        return x.rearrange("p (h n) -> p h n", h=n)

                    def spread(x, n, w):
                        return x.unsqueeze(2).to_broadcast([P, n, w])

                    def gain(i, n):
                        return gains[:, i:i + 1, :].to_broadcast([P, n, HD])

                    def select(n, rounds, rest):
                        for r in range(rounds):
                            link(dve.max(top8[:, :], acc[:, 0:n]))
                            if r == rounds - 1 and rest:
                                link(dve.memset(top8[:, rest:8], TAKEN))
                            link(dve.match_replace(acc[:, 0:n], top8[:, :], acc[:, 0:n], TAKEN))
                        link(dve.tensor_scalar(acc[:, 0:n], acc[:, 0:n], TAKEN / 2, NEG, ALU.is_gt, ALU.mult))

                    for st, *a in order:
                        if st == "nsum":
                            g, t = a
                            dve.wait_ge(pj_free, pj_use["proj", g, t, 0])
                            n = 5 if g == C else 8
                            dve.tensor_reduce(stats[:, 0:n], heads(sq[:, 0:n * HD], n), AX.X,
                                              ALU.add).then_inc(stats_in, 1)
                            own(stats_in)
                        elif st == "nmul":
                            g, t = a
                            n = g * NT + t
                            dve.wait_ge(rstd_out, n + 1)
                            if n:
                                dve.wait_ge(state_stored, 16 * n_states[STEPS[n - 1]])
                            if g in (A, D):
                                link(dve.tensor_tensor(heads(qk[:, :], 8), heads(z[:, 0:512], 8),
                                                       spread(rstd[:, 0:8], 8, HD), ALU.mult))
                                i = 0 if g == A else 4
                                dve.tensor_tensor(heads(qk[:, 0:256]), heads(qk[:, 0:256]), gain(i, 4), ALU.mult)
                                dve.tensor_tensor(heads(qk[:, 256:512]), heads(qk[:, 256:512]), gain(i + 1, 4),
                                                  ALU.mult).then_inc(qk_ready, 1)
                                own(qk_ready)
                            elif g == C:
                                link(dve.tensor_tensor(heads(qk[:, 0:320], 5), heads(z[:, 0:320], 5),
                                                       spread(rstd[:, 0:5], 5, HD), ALU.mult))
                                dve.tensor_tensor(heads(qk[:, 0:256]), heads(qk[:, 0:256]), gain(2, 4), ALU.mult)
                                dve.tensor_tensor(qk[:, 256:320], qk[:, 256:320], gains[:, 3, :],
                                                  ALU.mult).then_inc(qk_ready, 1)
                                own(qk_ready)
                            else:
                                dve.tensor_scalar(qk[:, 0:CQ], z[:, 0:CQ], rstd[:, 0:1], None, ALU.mult)
                                dve.scalar_tensor_tensor(out=kr[:, 0, :], in0=z[:, 512:544], scalar=rstd[:, 2:3],
                                                         in1=g_rope[:, 1, :], op0=ALU.mult, op1=ALU.mult)
                                dve.scalar_tensor_tensor(out=qk[:, CQ:512], in0=z[:, CQ:512], scalar=rstd[:, 1:2],
                                                         in1=g_ckv[:, :], op0=ALU.mult,
                                                         op1=ALU.mult).then_inc(qk_ready, 1)
                                own(qk_ready)
                        elif st == "nsum2":
                            (t,) = a
                            dve.wait_ge(pj_free, pj_use["upk", t])
                            sv = heads(sq[:, 0:384])
                            dve.tensor_reduce(stats[:, 8:12], sv[:, :, 0:64], AX.X, ALU.add)
                            dve.tensor_reduce(stats[:, 12:16], sv[:, :, 64:96], AX.X, ALU.add)
                            dve.tensor_reduce(stats[:, 16:20], heads(sq2[:, :]), AX.X,
                                              ALU.add).then_inc(stats2_in, 1)
                            own(stats2_in)
                        elif st == "nmul2":
                            (t,) = a
                            dve.wait_ge(rstd2_out, t + 1)
                            dve.tensor_tensor(bq[:, :, 0:64], bq[:, :, 0:64], spread(rstd[:, 8:12], 4, HD), ALU.mult)
                            dve.tensor_tensor(bq[:, :, 64:96], bq[:, :, 64:96], spread(rstd[:, 12:16], 4, RR),
                                              ALU.mult)
                            link(dve.tensor_tensor(bk[:, :, 0:64], bk[:, :, 0:64], spread(rstd[:, 16:20], 4, HD),
                                                   ALU.mult))
                            dve.tensor_tensor(bq[:, :, 0:64], bq[:, :, 0:64], gain(6, 4), ALU.mult)
                            dve.tensor_tensor(bk[:, :, 0:64], bk[:, :, 0:64], gain(7, 4), ALU.mult)
                            dve.tensor_tensor(bq[:, :, 64:96], bq[:, :, 64:96],
                                              g_rope[:, 0:1, :].to_broadcast([P, H, RR]),
                                              ALU.mult).then_inc(normed2, 1)
                            own(normed2)
                        elif st == "gate":
                            g, t = a
                            dve.wait_ge(pj_free, pj_use["proj", g, t, len(PIECES[g]) - 1])
                            link(dve.tensor_scalar(eg[:, :], eg[:, :], 1.0, None, ALU.add))
                            link(dve.reciprocal(eg[:, :], eg[:, :]))
                            dve.tensor_tensor(gate[:, (g * NT + t) % 2, :], z[:, 768:1024], eg[:, :],
                                              ALU.mult).then_inc(gated, 1)
                            own(gated)
                        elif st == "forget":
                            (t,) = a
                            dve.wait_ge(pj_free, pj_use["proj", D, t, 1])
                            if t:
                                dve.wait_ge(state_stored, 16 * n_states[D, t - 1])
                            link(dve.tensor_tensor(fl[:, 0, :], z[:, 512:516], b_f[:, :], ALU.add))
                            dve.tensor_scalar(fl[:, 4, :], fl[:, 0, :], 0.0, None, ALU.min)
                            dve.scalar_tensor_tensor(out=fl[:, 1, :], in0=fl[:, 0, :], scalar=-1.0, in1=fl[:, 0, :],
                                                     op0=ALU.mult, op1=ALU.max).then_inc(forget_in, 1)
                            own(forget_in)
                            dve.wait_ge(forget_in, t + 1)
                            dve.wait_ge(forget_ln, t + 1)
                            dve.tensor_tensor(fl[:, 5, :], fl[:, 4, :], fl[:, 3, :], ALU.subtract)
                            dve.tensor_tensor(fl[:, 6, :], fl[:, 3, :], fl[:, 4, :],
                                              ALU.subtract).then_inc(forget_out, 1)
                            own(forget_out)
                        elif st == "isc":
                            t, i = a
                            x, n = index_no(t, i), keys_of(C, t)
                            dve.wait_ge(idx_relu, x + 1)
                            if i:
                                dve.wait_ge(idx_added, x)
                                dve.scalar_tensor_tensor(out=acc[:, 0:n], in0=probs[:, x % 2, 0:n],
                                                         scalar=iw[:, t % 2, i:i + 1], in1=acc[:, 0:n],
                                                         op0=ALU.mult, op1=ALU.add).then_inc(idx_added, 1)
                                own(idx_added)
                            else:
                                dve.tensor_scalar(acc[:, 0:n], probs[:, x % 2, 0:n], iw[:, t % 2, i:i + 1], None,
                                                  ALU.mult).then_inc(idx_added, 1)
                                own(idx_added)
                        elif st == "select":
                            (t,) = a
                            n = keys_of(C, t)
                            if indexed(t):
                                dve.wait_ge(idx_added, index_no(t + 1, 0))
                                link(dve.memset(acc[0:64, n - 64:n], NEG))
                                select(n, TOPK_P // 8, 0)
                            else:
                                link(dve.memset(acc[:, 0:n], 0.0))
                                link(dve.memset(acc[0:64, n - 64:n], NEG))
                        elif st == "select8":
                            (p,) = a
                            dve.wait_ge(o_full, p + 1)
                            dve.tensor_copy(acc[:, 0:KEYS8], ob[:, 0:KEYS8]).then_inc(o_free, 1)
                            own(o_free)
                            dve.wait_ge(o_free, o_use["score8", p])
                            select(KEYS8, -(-TOPK_S // 8), TOPK_S % 8)
                        elif st in ("sm", "sm8"):
                            g, t, h = a if st == "sm" else (a[0], 8, a[1])
                            u = unit(g, t, h)
                            n = keys_of(g, t) if t < 8 else KEYS8
                            if t == 8 and g == D:
                                dve.wait_ge(past_loaded, 16 * past_dmas[D, h])
                                link(dve.tensor_scalar(nlf_row[:, 0:PAST], nlf_row[:, 0:PAST], -1.0, None, ALU.mult))
                                if h == 0:
                                    dve.wait_ge(t_full, t_use["tcum", 7])
                                    link(dve.memset(zero_row, 0.0))
                                link(dve.tensor_tensor_scan(nf8[:, :], nlf_row[:, :], zero_row, 0.0,
                                                            ALU.add, ALU.add))
                                link(dve.tensor_tensor(nf8[:, PAST:KEYS8], nf8[:, PAST:KEYS8], mask_new[:, :],
                                                       ALU.add))
                            if t < 8 and g == D and h == 0:
                                dve.wait_ge(t_free, t_use["tcum", t])
                            dve.wait_ge(s_full, u + 1)
                            dst, src, m = probs[:, u % 2, 0:n], sc[:, u % 2, 0:n], mx[:, u % 2:u % 2 + 1]
                            if g == B:
                                x = dve.tensor_scalar(dst, src, MLA_SCALE, None, ALU.mult, ALU.max, accum_out=m)
                            else:
                                if t == 8:
                                    bias = {A: bias_s[:, :], C: acc[:, 0:KEYS8], D: nf8[:, :]}[g]
                                else:
                                    bias = {A: band[:, h, BAND - n:BAND], C: acc[:, 0:n], D: nf[:, h, 0:n]}[g]
                                x = dve.tensor_tensor_reduce(dst, src, bias, 1.0, -3.4e38, ALU.add, ALU.max, m)
                            link(x)
                            dve.tensor_scalar(nmx[:, u % 2:u % 2 + 1], m, -1.0, None, ALU.mult).then_inc(row_max, 1)
                            own(row_max)
                        elif st == "tp8":
                            g, p = a
                            u = unit(g, 8, p)
                            dve.wait_ge(probs_ready, u + 1)
                            link(dve.reciprocal(rs[:, 0:1], sm[:, u % 4:u % 4 + 1]))
                            dve.tensor_scalar(probs[:, u % 2, 0:KEYS8], probs[:, u % 2, 0:KEYS8], rs[:, 0:1], None,
                                              ALU.mult).then_inc(probs_scaled, 1)
                            own(probs_scaled)
                        elif st == "pv8":
                            g, p = a
                            dve.wait_ge(pv_done, unit(g, 8, p) + 1)
                            if p == 0 and g:
                                dve.wait_ge(t_full, t_use["y8", g - 1, 8])
                            for h in range(H):
                                r = 64 * (h % 2)
                                src = ob[r:r + 64, 0:256].rearrange("p (b c n) -> p b c n", b=2, c=2)
                                x = dve.tensor_copy(
                                    ot8[r:r + 64, h // 2, 32 * p:32 * p + 32].rearrange("p (b n) -> p b n", b=2),
                                    src[:, :, h // 2, h * NQ:(h + 1) * NQ])
                                x.then_inc(ot_ready if h < H - 1 else o_free, 1)
                                own(ot_ready if h < H - 1 else o_free)
                        elif st == "y":
                            g, t = a
                            n = g * NT + t
                            dve.wait_ge(probs_ready, unit(g, t, 3) + 1)
                            link(dve.reciprocal(rs[:, :], sm[:, :]))
                            dve.wait_ge(pv_done, unit(g, t, 3) + 1)
                            if n:
                                dve.wait_ge(mix_stored, 16 * n)
                            dve.tensor_tensor(heads(mixt[:, t % 2, :]), heads(ob[:, 0:256]), spread(rs[:, :], 4, HD),
                                              ALU.mult).then_inc(o_free, 1)
                            own(o_free)
                            dve.wait_ge(o_free, o_use["pv", g, t])
                            dve.wait_ge(gated, n + 1)
                            dve.tensor_tensor(mixt[:, t % 2, :], mixt[:, t % 2, :], gate[:, (g * NT + t) % 2, :],
                                              ALU.mult).then_inc(mixed, 1)
                            own(mixed)
                        elif st == "y8":
                            g, t = a
                            n = g * NT + t
                            dve.wait_ge(t_free, t_use["y8", g, t])
                            dve.wait_ge(mix_stored, 16 * n)
                            dve.wait_ge(gated, n + 1)
                            dve.tensor_tensor(mixt[:, 0, :], y8[:, :], gate[:, (g * NT + t) % 2, :], ALU.mult).then_inc(mixed, 1)
                            own(mixed)
                        elif st == "pj_past":
                            k = ordinal[("pj_past", *a)]
                            dve.wait_ge(pj_free, pj_use[("pj_past", *a)])
                            dve.tensor_reduce(stats[:, 20:24], heads(sq2[:, :]), AX.X, ALU.add).then_inc(statsp_in, 1)
                            own(statsp_in)
                            dve.wait_ge(rstdp_out, k)
                            link(dve.tensor_tensor(heads(kp[:, :]), heads(kp[:, :]), spread(rstd[:, 20:24], 4, HD),
                                                   ALU.mult))
                            dve.tensor_tensor(heads(kp[:, :]), heads(kp[:, :]), gain(7, 4),
                                              ALU.mult).then_inc(past_normed, 1)
                            own(past_normed)

                @block.gpsimd
                def _(pool):
                    counts = {}

                    def own(s):
                        counts[s.name] = counts.get(s.name, 0) + 1
                        pool.wait_ge(s, counts[s.name])

                    
                    def link(ins):
                        ins.then_inc(pool_step, 1)
                        own(pool_step)

                    def inv_root(lo, hi):
                        link(pool.tensor_scalar(rstd[:, lo:hi], stats[:, lo:hi], EPS, None, ALU.add))
                        return pool.tensor_tensor(rstd[:, lo:hi], rstd[:, lo:hi], half[:, 0:hi - lo], ALU.pow)

                    def rotate(dst, x, n, w, table, t):
                        c = table[:, 0, t:t + 1, :].to_broadcast([P, n, w])
                        lo, hi = slice(0, w // 2), slice(w // 2, w)
                        s0 = table[:, 1, t:t + 1, lo].to_broadcast([P, n, w // 2])
                        s1 = table[:, 1, t:t + 1, hi].to_broadcast([P, n, w // 2])
                        u = rt[:, 0, 0:n * w].rearrange("p (n w) -> p n w", n=n)
                        v = rt[:, 1, 0:n * w].rearrange("p (n w) -> p n w", n=n)
                        link(pool.tensor_tensor(u, x, c, ALU.mult))
                        link(pool.tensor_tensor(v[:, :, lo], x[:, :, hi], s0, ALU.mult))
                        link(pool.tensor_tensor(v[:, :, hi], x[:, :, lo], s1, ALU.mult))
                        return pool.tensor_tensor(dst, u, v, ALU.add)

                    link(pool.memset(q_diag[:, :, :, :, :], 0.0))
                    link(pool.memset(iq_diag[:, :, :, :], 0.0))
                    for st, *a in order:
                        if st == "rstd":
                            g, t = a
                            if g == B:
                                pool.wait_ge(pj_free, pj_use["proj", B, t, 1])
                                x = inv_root(0, 3)
                            else:
                                pool.wait_ge(stats_in, ordinal["nsum", g, t])
                                x = inv_root(0, 5 if g == C else 8)
                            x.then_inc(rstd_out, 1)
                            own(rstd_out)
                        elif st == "rstd2":
                            pool.wait_ge(stats2_in, a[0] + 1)
                            inv_root(8, 20).then_inc(rstd2_out, 1)
                            own(rstd2_out)
                        elif st == "pj_past":
                            pool.wait_ge(statsp_in, ordinal[("pj_past", *a)])
                            inv_root(20, 24).then_inc(rstdp_out, 1)
                            own(rstdp_out)
                        elif st == "rope":
                            g, t = a
                            pool.wait_ge(qk_ready, ordinal["nmul", g, t])
                            if g == B:
                                rotate(kr[:, 1:2, :], kr[:, 0:1, :], 1, RR, rope_b, t).then_inc(roped, 1)
                                own(roped)
                            else:
                                x = qk[:, 0:320].rearrange("p (h n) -> p h n", h=5)[:, :, 0:16]
                                link(rotate(x, x, 5, 16, rope_c, t))
                                link(pool.tensor_copy(qk[:, 320:384], qk[:, 256:320]))
                                pool.wait_ge(pj_free, pj_use["proj", C, t, 1])
                                link(pool.tensor_copy(ik4[:, :, :], z[:, 640:672].unsqueeze(1)
                                                      .to_broadcast([P, 4, ID])))
                                pool.tensor_scalar(iw[:, t % 2, :], z[:, 672:680], IH ** -0.5, None,
                                                   ALU.mult).then_inc(roped, 1)
                                own(roped)
                        elif st == "rope2":
                            (t,) = a
                            pool.wait_ge(normed2, t + 1)
                            x = bq[:, :, 64:96]
                            link(rotate(x, x, H, RR, rope_b, t))
                            pool.wait_ge(roped, ordinal["rope", B, t])
                            if t < 8:
                                pool.tensor_copy(bk[:, :, 64:96], kr[:, 1:2, :].to_broadcast([P, H, RR])
                                                 ).then_inc(roped2, 1)
                                own(roped2)
                            else:
                                def part(c, n, w):
                                    return z[:, c:c + n * w].rearrange("p (n w) -> p n w", n=n)
                                link(pool.tensor_copy(part(0, H, HD), bq[:, :, 0:HD]))
                                link(pool.tensor_copy(part(256, H, RR), bq[:, :, HD:96]))
                                link(pool.tensor_copy(part(384, H, HD), bk[:, :, 0:HD]))
                                pool.tensor_copy(part(640, H, RR), kr[:, 1:2, :].to_broadcast([P, H, RR])
                                                 ).then_inc(roped2, 1)
                                own(roped2)
                        elif st == "widen":
                            (t,) = a
                            pool.wait_ge(forget_out, t + 1)
                            pool.tensor_copy(lfw[:, :, :], fl[:, 6, :].unsqueeze(2)
                                             .to_broadcast([P, H, P])).then_inc(forget_wide, 1)
                            own(forget_wide)
                        elif st == "q_diag":
                            g, p = a
                            pool.wait_ge(t_free, t_use[LAST_TURN[g], g, 8])
                            if p >= 2:
                                pool.wait_ge(s_full, unit(g, 8, p - 2) + 1)
                            pack = slice(32 * p, 32 * p + 32)
                            parts = []
                            for h in range(H):
                                r = 64 * (h % 2)
                                parts.append((
                                    q_diag[r:r + 64, p % 2, h // 2, :, h * NQ:(h + 1) * NQ],
                                    qt[r:r + 64, 0, h // 2, pack].rearrange("p (b n) -> p b n", b=2)))
                                if g == B:
                                    parts.append((
                                        q_diag[32 * h:32 * h + 32, p % 2, 2, :, h * NQ:(h + 1) * NQ],
                                        qt[32 * h:32 * h + 32, 0, 2, pack].rearrange("p (b n) -> p b n", b=2)))
                            for dst, src in parts[:-1]:
                                link(pool.tensor_copy(dst, src))
                            pool.tensor_copy(*parts[-1]).then_inc(q_diag_ready, 1)
                            own(q_diag_ready)
                        elif st == "iq_diag":
                            (p,) = a
                            if p:
                                pool.wait_ge(idx_full, IDX8 + 2 * p)
                                pool.wait_ge(o_full, p)
                            for ih in range(IH):
                                r = 32 * (ih % 4)
                                x = pool.tensor_copy(
                                    iq_diag[r:r + 32, ih // 4, :, ih * NQ:(ih + 1) * NQ],
                                    iqt[r:r + 32, 0, ih // 4, 32 * p:32 * p + 32].rearrange("p (b n) -> p b n", b=2))
                                if ih < IH - 1:
                                    link(x)
                            x.then_inc(iq_diag_ready, 1)
                            own(iq_diag_ready)
                            if p == 0:
                                pool.wait_ge(side_loaded, 16 * IH)
                            for b2 in range(2):
                                x = pool.tensor_scalar(wsel[:, b2, :], pick[:, :],
                                                       iw_rows[:, 2 * p + b2:2 * p + b2 + 1], None, ALU.mult)
                            x.then_inc(wsel_ready, 1)
                            own(wsel_ready)
            clear_sems()

            with ExitStack() as mem, nc.Block() as block:
                def s3(name, shape, dt=F32):
                    return mem.enter_context(nc.sbuf_tensor(name, shape, dt))
                SLOTS = 4
                w_out = xn_t[:, :, :].rearrange("p c n -> p (c n)")[:, 0:KC * DM].rearrange("p (c n) -> p c n", c=KC)
                w_all = w_buf[:, :, :].rearrange("p c n -> p (c n)")
                w_gate = w_all[:, 0:KC * DM].rearrange("p (c n) -> p c n", c=KC)
                w_ple = w_all[:, KC * DM:KC * DM + 2 * DM].rearrange("p (c n) -> p c n", c=2)
                mi = s3("mi", [P, SLOTS, DM])
                xi = s3("xi", [P, SLOTS, DM])
                p_t = s3("p_t", [P, SLOTS, 2, P])
                mi_t = s3("mi_t", [P, KC, P])
                xn3 = s3("xn3", [P, DM])
                xn3_t = s3("xn3_t", [P, KC, P])
                sg = s3("sg", [P, DM])
                st3 = s3("st3", [P, 2 * NT])

                @block.sync
                def _(sp):
                    def load(t):
                        if t >= SLOTS:
                            sp.wait_ge(x2_stored, 16 * (t - SLOTS + 1))
                        sp.dma_start(mi[:, t % SLOTS, :], mixd[t]).then_inc(mix_in, 16)
                        sp.dma_start(xi[:, t % SLOTS, :], lay(xs, layer)[t]).then_inc(x_in, 16)
                        sp.dma_start(p_t[:, t % SLOTS, :, :], lay(ins["p_t"], layer)[t]).then_inc(p_in, 16)
                        sp.wait_ge(mix_in, 16 * (t + 1))
                        sp.wait_ge(x_in, 16 * (t + 1))
                        sp.wait_ge(p_in, 16 * (t + 1))
                    for w, name in ((w_out, "w_out"), (w_gate, "w_gate"), (w_ple, "w_ple")):
                        sp.dma_start(w, lay(ins[name], layer).rearrange("(c p) n -> p c n", p=P)).then_inc(out_w, 16)
                    for t in range(SLOTS):
                        load(t)
                    for t in range(NT):
                        sp.wait_ge(x2_ready, t + 1)
                        sp.dma_start(xs[bass.ds(layer + 1, 1), :, :, :].rearrange("a t p n -> (a t) p n")[t],
                                     xi[:, t % SLOTS, :]).then_inc(x2_stored, 16)
                        if t + SLOTS < NT:
                            load(t + SLOTS)
                    sp.wait_ge(x2_stored, 16 * NT)

                turns3 = []
                for t in range(NT + 1):
                    if t < NT:
                        turns3 += [("m", t, 0), ("m", t, 1)]
                    if t >= 1:
                        turns3 += [("x", t - 1, 0), ("x", t - 1, 1)]
                turn3 = {k: i + 1 for i, k in enumerate(turns3)}

                @block.tensor
                def _(pe):
                    def turn(key, src):
                        n = turn3[key]
                        if n > 2:
                            pe.wait_ge(t_free, n - 2)
                        for k in range(4):
                            c = 4 * key[2] + k
                            m = nc.tensor.transpose(tb[:, (n - 1) % 2, k * P:(k + 1) * P], src[:, c * P:(c + 1) * P],
                                                    ident[:, :])
                        m.then_inc(t_full, 1)

                    def product(banks, lhs, w, nk, done):
                        for j in range(2):
                            for k in range(nk):
                                m = nc.tensor.matmul(banks[j], lhs[:, k, :], w[:, k, j * 512:(j + 1) * 512],
                                                     start=k == 0, stop=k == nk - 1)
                        m.then_inc(done, 1)

                    pe.wait_ge(out_w, 48)
                    for t in range(NT + 1):
                        if t < NT:
                            pe.wait_ge(mix_in, 16 * (t + 1))
                            for j in range(2):
                                turn(("m", t, j), mi[:, t % SLOTS, :])
                            if t:
                                pe.wait_ge(x1_ready, t)
                            pe.wait_ge(t_free, turn3["m", t, 1])
                            product([sc[:, 0, 0:512], sc[:, 0, 512:1024]], mi_t, w_out, KC, a_full)
                        if t >= 1:
                            s = t - 1
                            if s:
                                pe.wait_ge(x2_ready, s)
                            pe.wait_ge(p_in, 16 * (s + 1))
                            product([pj[:, :], ob[:, :]], p_t[:, s % SLOTS, :, :], w_ple, 2, c_full)
                            pe.wait_ge(xn_ready, s + 1)
                            for j in range(2):
                                turn(("x", s, j), xn3[:, :])
                            pe.wait_ge(t_free, turn3["x", s, 1])
                            if s:
                                pe.wait_ge(sg_exp, s)
                            product([sc[:, 1, 0:512], sc[:, 1, 512:1024]], xn3_t, w_gate, KC, b_full)

                @block.scalar
                def _(act):
                    counts = {}

                    def own(s):
                        counts[s.name] = counts.get(s.name, 0) + 1
                        act.wait_ge(s, counts[s.name])

                    for t in range(NT + 1):
                        if t < NT:
                            for j in range(2):
                                n = turn3["m", t, j]
                                act.wait_ge(t_full, n)
                                if t and j == 0:
                                    act.wait_ge(a_full, t)
                                act.activation(mi_t[:, 4 * j:4 * j + 4, :],
                                               tb[:, (n - 1) % 2, :].rearrange("p (k n) -> p k n", k=4),
                                               ACT.Copy).then_inc(t_free, 1)
                                own(t_free)
                        if t >= 1:
                            s = t - 1
                            for j in range(2):
                                n = turn3["x", s, j]
                                act.wait_ge(t_full, n)
                                for k in range(4):
                                    c = 4 * j + k
                                    a = act.activation(xn3_t[:, c, :], tb[:, (n - 1) % 2, k * P:(k + 1) * P], ACT.Copy,
                                                       scale=g_ple_c[:, c:c + 1])
                                a.then_inc(t_free, 1)
                                own(t_free)
                            if s:
                                act.wait_ge(x2_ready, s)
                            act.wait_ge(b_full, s + 1)
                            act.activation(sg[:, :], sc[:, 1, :], ACT.Exp, scale=-1.0).then_inc(sg_exp, 1)
                            own(sg_exp)

                @block.gpsimd
                def _(pool):
                    counts = {}

                    def own(s):
                        counts[s.name] = counts.get(s.name, 0) + 1
                        pool.wait_ge(s, counts[s.name])

                    for t in range(NT):
                        pool.wait_ge(x_squared, t + 1)
                        pool.tensor_scalar(st3[:, NT + t:NT + t + 1], st3[:, t:t + 1], EPS, None,
                                           ALU.add).then_inc(pool_step, 1)
                        own(pool_step)
                        pool.wait_ge(pool_step, t + 1)
                        pool.tensor_tensor(st3[:, NT + t:NT + t + 1], st3[:, NT + t:NT + t + 1],
                                           half[:, 0:1], ALU.pow).then_inc(x_rstd, 1)
                        own(x_rstd)

                @block.vector
                def _(dve):
                    counts = {}

                    def own(s):
                        counts[s.name] = counts.get(s.name, 0) + 1
                        dve.wait_ge(s, counts[s.name])

                    def link(ins):
                        ins.then_inc(dve_step, 1)
                        own(dve_step)

                    for t in range(NT + 1):
                        if t < NT:
                            dve.wait_ge(a_full, t + 1)
                            dve.wait_ge(x_in, 16 * (t + 1))
                            dve.tensor_tensor(xi[:, t % SLOTS, :], xi[:, t % SLOTS, :], sc[:, 0, :],
                                              ALU.add).then_inc(x1_ready, 1)
                            own(x1_ready)
                            dve.wait_ge(x1_ready, t + 1)
                            if t:
                                dve.wait_ge(t_full, turn3["x", t - 1, 1])
                            dve.scalar_tensor_tensor(out=xn3[:, :], in0=xi[:, t % SLOTS, :], scalar=1.0 / DM,
                                                     in1=xi[:, t % SLOTS, :], op0=ALU.mult, op1=ALU.mult,
                                                     accum_out=st3[:, t:t + 1]).then_inc(x_squared, 1)
                            own(x_squared)
                        if t >= 1:
                            s = t - 1
                            dve.wait_ge(sg_exp, s + 1)
                            link(dve.tensor_scalar(sg[:, :], sg[:, :], 1.0, None, ALU.add))
                            link(dve.reciprocal(sg[:, :], sg[:, :]))
                            dve.wait_ge(c_full, s + 1)
                            dve.tensor_tensor(sg[:, 0:512], sg[:, 0:512], pj[:, :], ALU.mult)
                            link(dve.tensor_tensor(sg[:, 512:1024], sg[:, 512:1024], ob[:, :], ALU.mult))
                            dve.tensor_tensor(xi[:, s % SLOTS, :], xi[:, s % SLOTS, :], sg[:, :],
                                              ALU.add).then_inc(x2_ready, 1)
                            own(x2_ready)
                        if t < NT:
                            dve.wait_ge(x_rstd, t + 1)
                            dve.tensor_scalar(xn3[:, :], xi[:, t % SLOTS, :], st3[:, NT + t:NT + t + 1], None,
                                              ALU.mult).then_inc(xn_ready, 1)
                            own(xn_ready)
            clear_sems()


def kernel(**inputs):
    import numpy as np
    import concourse.bacc as bacc
    from concourse.bass_utils import run_bass_kernel_spmd

    f32 = np.float32
    a = {k: np.asarray(v) for k, v in inputs.items()}
    L = DEPTH

    def rows(prompt, sample):
        lead = prompt.shape[:-3]
        w = prompt.shape[-1]
        return np.concatenate([prompt.reshape(lead + (TP, P, w)), sample.reshape(lead + (1, P, w))], axis=-3)

    pos = np.concatenate([np.arange(TP * P), PAST + np.tile(np.arange(NQ), NB)]).reshape(NT, P)

    def rope(width):
        n = width // 2
        inv = f32(500000.0) ** (-np.arange(n, dtype=f32) / f32(n))
        ang = pos.astype(f32)[:, :, None] * inv[None, None, :]
        c, s = np.cos(ang), np.sin(ang)
        both = np.stack([np.concatenate([c, c], -1), np.concatenate([-s, s], -1)])
        return np.ascontiguousarray(both.transpose(2, 0, 1, 3)).astype(f32)

    i, w = np.arange(P)[:, None], np.arange(BAND)[None, :]
    rel_p = np.clip(i + 512 - w, -128, 128) + 128
    q, k = np.arange(NQ)[:, None], np.arange(KEYS8)[None, :]
    rel_s = np.clip(q + PAST - k, -128, 128) + 128
    rb = a["a_rel_bias"]
    new = np.where(np.arange(NQ)[None, :] > np.arange(NQ)[:, None], f32(NEG), f32(0.0)).astype(f32)
    t = lambda x, *axes: x.transpose(*axes)
    ins = {
        "x0": rows(a["x_prompt"][None], a["x_sample"][None])[0],
        "tri": np.triu(np.ones((P, P), f32)),
        "mask_new": np.tile(new, (8, 1)),
        "pick": np.tile(np.eye(NQ, dtype=f32), (IH, H)),
        "rope_b": rope(RR), "rope_c": rope(16),
        "g_in": t(a["g_in"].reshape(L, KC, P), 0, 2, 1),
        "g_ple": t(a["g_ple"].reshape(L, KC, P), 0, 2, 1),
        "g_cq": t(a["b_g_cq"].reshape(L, 3, P), 0, 2, 1),
        "g_qk": a["g_qk"], "g_ckv": a["b_g_ckv"], "g_rope": a["g_rope"], "b_f": a["d_b_f"],
        "w_in": a["w_in"], "w_uq": a["b_w_uq"], "w_ukv": a["b_w_ukv"],
        "w_out": a["w_out"], "w_gate": a["w_ple_gate"], "w_ple": a["w_ple_proj"],
        "bias_p": t(rb[:, :, rel_p], 0, 2, 1, 3),
        "bias_s": np.tile(rb[:, :, rel_s].reshape(L, H * NQ, KEYS8), (1, 2, 1)),
        "p_t": t(rows(a["p_prompt"], a["p_sample"][:, None]).reshape(L, NT, P, 2, P), 0, 1, 4, 3, 2),
        "a_v": a["cache_a_v"].reshape(L, NB, PAST, GW), "d_v": a["cache_d_v"].reshape(L, NB, PAST, GW),
        "a_kt": t(a["cache_a_k"].reshape(L, NB, PAST, 2, P), 0, 3, 4, 1, 2),
        "d_kt": t(a["cache_d_k"].reshape(L, NB, PAST, 2, P), 0, 3, 4, 1, 2),
        "c_kt": t(a["cache_c_k"], 0, 3, 1, 2), "c_v": a["cache_c_v"], "c_ikt": t(a["cache_c_idx_k"], 0, 3, 1, 2),
        "b_ckvt": t(a["cache_b_ckv"], 0, 3, 1, 2), "b_krt": t(a["cache_b_krope"], 0, 3, 1, 2),
        "d_lft": t(a["cache_d_logf"], 0, 1, 3, 2),
    }
    ins = {k: np.ascontiguousarray(v) for k, v in ins.items()}
    outs = {"xs": (L + 1, NT, P, DM), "a_k": (L, 5, P, GW), "a_v": (L, 5, P, GW), "b_ckv": (L, NT, P, CKV),
            "b_kr": (L, NT, P, RR), "c_k": (L, NT, P, HD), "c_v": (L, NT, P, HD), "c_ik": (L, NT, P, ID),
            "d_k": (L, NT, P, GW), "d_v": (L, NT, P, GW), "d_lf": (L, NT, P, H)}
    nc = bacc.Bacc("TRN2", target_bir_lowering=False, num_devices=1)
    din = {k: nc.dram_tensor("in_" + k, v.shape, F32, kind="ExternalInput").ap() for k, v in ins.items()}
    dout = {k: nc.dram_tensor("out_" + k, s, F32, kind="ExternalOutput").ap() for k, s in outs.items()}
    scratch = {"xs": dout["xs"],
               "mix": nc.dram_tensor("mix_scratch", (NT, P, DM), F32, kind="Internal").ap(),
               "iw": nc.dram_tensor("iw_scratch", (P, IH), F32, kind="Internal").ap(),
               "lf": nc.dram_tensor("lf_scratch", (H, P), F32, kind="Internal").ap()}
    build(nc, din, dout, scratch)
    r = run_bass_kernel_spmd(nc, [{"in_" + k: v for k, v in ins.items()}], core_ids=[0]).results[0]
    o = {k: r["out_" + k] for k in outs}

    def prompt(name, tail):
        x = o[name][:, :-1]
        return x.reshape((L, 1, x.shape[1] * P) + tail)

    def sample(name, tail):
        return o[name][:, -1].reshape((L, NB, NQ) + tail)

    tails = [("a_k", (H, HD)), ("a_v", (H, HD)), ("b_ckv", (CKV,)), ("b_kr", (RR,)), ("c_k", (HD,)), ("c_v", (HD,)),
             ("c_ik", (ID,)), ("d_k", (H, HD)), ("d_v", (H, HD)), ("d_lf", (H,))]
    return (o["xs"][L, :TP].reshape(1, TP * P, DM), o["xs"][L, TP].reshape(NB, NQ, DM),
            *[prompt(n, s) for n, s in tails], *[sample(n, s) for n, s in tails])
```

```python
from contextlib import ExitStack

import concourse.bass as bass
from concourse import mybir

ALU = mybir.AluOpType
ACT = mybir.ActivationFunctionType
F32 = mybir.dt.float32
BF16 = mybir.dt.bfloat16
F32R = mybir.dt.float32r
AX = mybir.AxisListType

P = 128
DM = 1024
KC = DM // P
DEPTH = 2
NT = 9
TP = 8
H, HD = 4, 64
GW = H * HD
NB, NQ, PAST = 8, 16, 256
KEYS8 = PAST + NQ
PACKS = NB // 2
A, B, C, D = range(4)
EPS = 1e-6
NEG = -1e30
TAKEN = -3e38
TOPK_P, TOPK_S = 256, KEYS8 // 4
MLA_SCALE = 96.0 ** -0.5
IH, ID = 8, 32
CQ, CKV, RR = 384, 128, 32
CHUNKS = [(0, 512, 0), (512, 512, 1),
          (2208, 296, 2),
          (1024, 512, 0), (1536, 288, 1),
          (1824, 320, 2), (2144, 320, 0),
          (2760, 512, 1), (3272, 516, 0)]
INDEX_CHUNK = 2
BUF_COLS = [516, 512, 320]
C_V_COL, C_GATE_COL = 2144, 2504
PIECES = {A: [(0, 0, 512), (1, 0, 512)], B: [(3, 0, 512), (4, 0, 288)],
          C: [(5, 0, 320), (6, 0, 320)], D: [(7, 0, 512), (8, 0, 260), (8, 260, 256)]}
STEPS = [(g, t) for g in range(4) for t in range(NT)]
BAND = 640


def first_key_tile(g, t):
    return max(0, t - 4) if g == A else 0


def keys_of(g, t):
    return (t + 1 - first_key_tile(g, t)) * P


def unit(g, t, i=0):
    return (g * NT + t) * 4 + i


LAST_TURN = {A: "tqk", B: "tk", C: "tqk", D: "tqk"}


def load_ordinal(ci):
    return sum(CHUNKS[c][2] == CHUNKS[ci][2] for c in range(3, ci + 1))


def next_in_buffer(ci):
    return next((c for c in range(ci + 1, len(CHUNKS)) if CHUNKS[c][2] == CHUNKS[ci][2]), None)


def mask_at(t):
    return 4096 - sum(keys_of(C, u) // 2 for u in range(3, t + 1))


def indexed(t):
    return keys_of(C, t) > TOPK_P


def index_turns(t):
    return 3 if t < TP and indexed(t) else 1


def halves(t):
    return -(-keys_of(C, t) // 512)


def index_no(t, i, j=0):
    return sum(IH * halves(u) for u in range(2, t)) + i * halves(t) + j


BEHIND = {A: 13, (A, 8): 30, B: 25, (B, 8): 30, C: 15}
ROUNDS = 1


def indexing():
    o, picks = [], []
    for t in range(NT):
        scores = [(0, ("iproj", t)), (0, ("irows", t))]
        scores += [(0.1, ("tix", t, b)) for b in range(index_turns(t))]
        if t < TP:
            scores.append((0, ("isplit", t)))
        else:
            o.extend(scores + [(0, ("side", C))])
            continue
        if indexed(t):
            scores += [(0.9, ("isc", t, i, j)) for i in range(IH) for j in range(halves(t))]
        n = len(scores)
        for k, x in enumerate(scores):
            o.append(x)
            upto = (k + 1) * len(picks) // n - k * len(picks) // n
            o.extend(picks[k * len(picks) // n:][:upto])
        picks = [(ROUNDS * keys_of(C, t) / 480.0, ("pick", t, r))
                 for r in range(TOPK_P // 8 // ROUNDS)] if indexed(t) else []
    o.extend(picks)
    return o


def pe_time(key):
    st, *a = key
    if st == "proj":
        return PIECES[a[0]][a[2]][2] * KC / 600.0
    if st in ("sc", "tp", "pv"):
        return keys_of(a[0], a[1]) / {"sc": 600.0, "tp": 1000.0, "pv": 1000.0}[st]
    return {"upq": 2.0, "upk": 0.9, "tqk": 0.5, "tq": 0.5, "tk": 0.5, "tlat": 0.5, "pj_past": 1.0,
            "t_past": 0.5, "sc8": 2.0, "tp8": 0.5, "pv8": 2.0}.get(st, 0.0)


def picks_first(keys):
    out = []
    for key in keys:
        at = len(out)
        while key[0] == "pick" and at and out[at - 1][0] != "pick" and out[at - 1][1] not in (key[1], C):
            at -= 1
        out.insert(at, key)
    return out


def schedule():
    done, o = [], []
    behind = indexing()

    def project(g, t, i):
        o.append(("proj", g, t, i))
        c, col, n = PIECES[g][i]
        if t == 8 and col + n == CHUNKS[c][1] and next_in_buffer(c):
            o.append(("load_w", next_in_buffer(c)))

    def spread_index(budget):
        mine = []
        while behind and budget > 0:
            cost, key = behind.pop(0)
            mine.append(key)
            if key == ("iproj", 8):
                mine.append(("load_w", next_in_buffer(INDEX_CHUNK)))
            budget -= cost
        whole, passed, taken = sum(map(pe_time, o)), 0, 0
        for key in o:
            done.append(key)
            passed += pe_time(key)
            upto = int(passed / whole * len(mine) + 1e-6)
            done.extend(picks_first(mine[taken:upto]))
            taken = upto
        done.extend(mine[taken:])
        o.clear()

    def norms(g, t, part):
        if (part == 0) != (g == B):
            if g != B:
                o.append(("nsum", g, t))
            o.append(("rstd", g, t))
        if part == 1:
            o.append(("nmul", g, t))
            if g in (B, C):
                o.append(("rope", g, t))

    def latents(g, t):
        if g == B:
            o.extend([("tlat", t), ("upq", t), ("upk", t)])

    def late(g, t):
        if g == B:
            o.extend([("nsum2", t), ("rstd2", t), ("nmul2", t), ("rope2", t)])
        if g == D:
            o.append(("forget", t))
            if t < 8:
                o.append(("widen", t))

    def turns(g, t):
        o.extend({A: [("tqk", g, t)], B: [("tq", g, t), ("tk", g, t)], C: [("tqk", g, t)],
                  D: [("tqk", g, t), ("tcum", t)]}[g])

    def finish(g, t):
        o.append(("gate", g, t))
        turns(g, t)
        o.append(("states", g, t))

    for i in range(len(PIECES[A])):
        project(A, 0, i)
    norms(A, 0, 0)
    norms(A, 0, 1)
    finish(A, 0)
    for n, (g, t) in enumerate(STEPS):
        nx = STEPS[n + 1] if n + 1 < len(STEPS) else None
        pieces = len(PIECES[nx[0]]) if nx else 0

        def softmax(h):
            o.extend([("sc", g, t, h), ("sm", g, t, h)])
        if t < 8:
            softmax(0)
            if nx[0] == B:
                project(*nx, 0)
                softmax(1)
                project(*nx, 1)
                norms(*nx, 0)
                norms(*nx, 1)
                o.append(("tp", g, t, 0))
                softmax(2)
                o.append(("pv", g, t, 0))
                latents(*nx)
                o.append(("tp", g, t, 1))
                softmax(3)
                o.append(("pv", g, t, 1))
                late(*nx)
                o.extend([("tp", g, t, 2), ("pv", g, t, 2), ("tp", g, t, 3), ("gate", *nx)])
                turns(*nx)
                o.append(("pv", g, t, 3))
            else:
                softmax(1)
                project(*nx, 0)
                o.append(("tp", g, t, 0))
                softmax(2)
                o.append(("pv", g, t, 0))
                norms(*nx, 0)
                project(*nx, 1)
                o.append(("tp", g, t, 1))
                softmax(3)
                o.append(("pv", g, t, 1))
                norms(*nx, 1)
                late(*nx)
                o.append(("tp", g, t, 2))
                if pieces > 2:
                    project(*nx, 2)
                o.extend([("pv", g, t, 2), ("tp", g, t, 3), ("gate", *nx)])
                turns(*nx)
                o.append(("pv", g, t, 3))
            o.extend([("y", g, t), ("states", *nx)])
        else:
            def before(p):
                if p >= PACKS:
                    return []
                b = [("q_diag", g, p)]
                if g == B:
                    blocks = [(p, b2, blk) for b2 in range(2) for blk in range(2)]
                    b += [("pj_past", *blocks[0])]
                    for m in range(1, 4):
                        b += [("pj_past", *blocks[m]), ("t_past", *blocks[m - 1])]
                    b += [("t_past", *blocks[3])]
                if g == C:
                    b += [("iq_diag", p), ("isc8", p, 0), ("isc8", p, 1), ("score8", p), ("select8", p)]
                return b
            if g == D:
                o.append(("side", g))
            o.extend([("load_pack", g, 0), ("load_pack", g, 1), *before(0)])
            if g == D:
                o.append(("load_out",))
            for p in range(PACKS):
                o.extend([("sc8", g, p), ("sm8", g, p)])
                b = before(p + 1)
                c1, c2 = {A: (1, 1), B: (3, 6), C: (2, 4), D: (1, 1)}[g]
                o.extend(b[:c1])
                if p < pieces:
                    project(*nx, p)
                if g == C:
                    o.extend([*b[c1:c2], ("tp8", g, p)])
                else:
                    o.extend([("tp8", g, p), *b[c1:c2]])
                if nx and p < 2:
                    norms(*nx, p)
                o.append(("pv8", g, p))
                o.extend(b[c2:])
                if p + 2 < PACKS:
                    o.append(("load_pack", g, p + 2))
            o.append(("y8", g, t))
            if nx:
                latents(*nx)
                late(*nx)
                finish(*nx)
        spread_index(BEHIND.get((g, t), BEHIND.get(g, 0)))
    assert not behind
    return done


def count_uses(order):
    ordinal, kinds, pj, tb, ob = {}, {}, {}, {}, {}
    for key in order:
        st = key[0]
        kinds[st] = kinds.get(st, 0) + 1
        ordinal[key] = kinds[st]
        if st in ("proj", "iproj", "upq", "upk", "pj_past"):
            pj[key] = len(pj) + 1
        if st in ("tlat", "tqk", "tix", "isc", "tq", "tk", "tcum", "tp8", "t_past", "y8"):
            tb[key] = len(tb) + 1
        if st == "tp":
            for j in range(-(-keys_of(key[1], key[2]) // 512)):
                tb[key + (j,)] = len(tb) + 1
        if st in ("score8", "pv8"):
            ob[key] = len(ob) + 1
        if st == "pv" and key[3] == 0:
            ob[key[:3]] = len(ob) + 1
    return ordinal, pj, tb, ob


def count_dmas():
    past, states, n, m = {}, {}, [0, 0], 0
    for g in range(4):
        for p in range(PACKS):
            n[p % 2] += {A: 3, B: 3, C: 5, D: 6}[g]
            past[g, p] = n[p % 2]
        for t in range(NT):
            m += {A: 2 if t >= 4 else 0, B: 2, C: 2, D: 3}[g]
            states[g, t] = m
    return past, states


def build(nc, ins, outs, scratch):
    with ExitStack() as ctx:
        def sb(name, shape, dt=F32):
            return ctx.enter_context(nc.sbuf_tensor(name, shape, dt))

        def ps(name, shape, dt=F32):
            return ctx.enter_context(nc.psum_tensor(name, shape, dt))

        all_sems = []

        def sem(name):
            s = ctx.enter_context(nc.semaphore(name))
            all_sems.append(s)
            return s

        ident = sb("ident", [P, P])
        ident_h = sb("ident_h", [P, P], BF16)
        tri = sb("tri", [P, P])
        mask_chunk = sb("mask_chunk", [P, P], BF16)
        mask_causal = sb("mask_causal", [P, P], BF16)
        mask_new = sb("mask_new", [P, NQ])
        pick = sb("pick", [P, 64])
        rope_b = sb("rope_b", [P, 2, NT, 32])
        rope_c = sb("rope_c", [P, 2, NT, 16])
        half = sb("half", [P, 16])
        g_in_c = sb("g_in_c", [P, KC])
        g_ple_c = sb("g_ple_c", [P, KC])
        g_cq_c = sb("g_cq_c", [P, 3])
        gains = sb("gains", [P, 8, HD])
        g_ckv = sb("g_ckv", [P, CKV])
        g_rope = sb("g_rope", [P, 2, RR])
        b_f = sb("b_f", [P, H])
        w_uq = sb("w_uq", [P, 3, 384])
        w_ukv = sb("w_ukv", [P, 512])
        xn_t = sb("xn_t", [P, KC, NT * P])
        w_buf = sb("w_buf", [P, KC * sum(BUF_COLS)])
        ct = sb("ct", [P, H * 1024])
        bias_s = sb("bias_s", [P, KEYS8])
        nf = ct[:, :].rearrange("p (h n) -> p h n", h=H)
        band = ct[:, 0:H * BAND].rearrange("p (h n) -> p h n", h=H)

        def chunk_view(ci):
            col, w, buf = CHUNKS[ci]
            start = KC * sum(BUF_COLS[:buf])
            return w_buf[:, start:start + KC * w].rearrange("p (c n) -> p c n", c=KC)

        def load_chunk(sp, l, ci, signal):
            col, w, buf = CHUNKS[ci]
            col2, cut = (C_GATE_COL, 64) if col == C_V_COL else (col + w // 2, w // 2)
            for c0, lo, hi in ((col, 0, cut), (col2, cut, w)):
                sp.dma_start(chunk_view(ci)[:, :, lo:hi], lay(ins["w_in"], l)[:, c0:c0 + hi - lo]
                             .rearrange("(c p) n -> p c n", p=P)).then_inc(signal, 16)

        w_out = xn_t[:, :, :].rearrange("p c n -> p (c n)")[:, 0:KC * DM].rearrange("p (c n) -> p c n", c=KC)
        w_gate = w_buf[:, 0:KC * DM].rearrange("p (c n) -> p c n", c=KC)
        w_ple = w_buf[:, KC * DM:(KC + 2) * DM].rearrange("p (c n) -> p c n", c=2)

        pj = ps("pj", [P, 512])
        tb = ps("tb", [P, 2, 512])
        ob = ps("ob", [P, 512])
        sc = ps("sc", [P, 2, 1024])

        xs, mixd = scratch["xs"], scratch["mix"]

        def lay(ap, l):
            dims = " ".join(f"d{i}" for i in range(1, ap.ndim))
            names = dims.split()
            if len(names) == 1:
                return ap[bass.ds(l, 1), :].rearrange("a b -> (a b)")
            idx = (bass.ds(l, 1),) + (slice(None),) * (ap.ndim - 1)
            return ap[idx].rearrange(f"a {dims} -> (a {names[0]}) {' '.join(names[1:])}")

        s_load = sem("const_loaded")
        s_copy = sem("x_copied")
        s_id = sem("ident_built")

        with nc.Block() as block:
            @block.sync
            def _(sp):
                sp.dma_start(xs[0], ins["x0"]).then_inc(s_copy, 16)
                for dst, src in ((tri, "tri"), (mask_new, "mask_new"), (pick, "pick")):
                    sp.dma_start(dst[:, :], ins[src]).then_inc(s_load, 16)
                sp.dma_start(rope_b[:, :, :, :], ins["rope_b"]).then_inc(s_load, 16)
                sp.dma_start(rope_c[:, :, :, :], ins["rope_c"]).then_inc(s_load, 16)
                sp.wait_ge(s_load, 5 * 16)
                sp.wait_ge(s_copy, 16)

            @block.gpsimd
            def _(pool):
                counts = {}

                def own(s):
                    counts[s.name] = counts.get(s.name, 0) + 1
                    pool.wait_ge(s, counts[s.name])

                pool.memset(half[:, :], -0.5).then_inc(s_id, 1)
                own(s_id)
                pool.memset(ident[:, :], 0.0).then_inc(s_id, 1)
                own(s_id)
                pool.memset(ident_h[:, :], 0.0).then_inc(s_id, 1)
                own(s_id)
                pool.memset(mask_chunk[:, :], 0.0).then_inc(s_id, 1)
                own(s_id)
                pool.memset(mask_causal[:, :], 0.0).then_inc(s_id, 1)
                own(s_id)
                pool.wait_ge(s_id, 5)
                for m in (ident, ident_h):
                    pool.affine_select(out=m[:, :], in_=m[:, :], compare_op=ALU.not_equal, fill=1.0, base=0,
                                       pattern=[[-1, P]], channel_multiplier=1).then_inc(s_id, 1)
                    own(s_id)
                pool.affine_select(out=mask_causal[:, :], in_=mask_causal[:, :], compare_op=ALU.is_ge, fill=NEG,
                                   base=0, pattern=[[-1, P]], channel_multiplier=1).then_inc(s_id, 1)
                own(s_id)
                pool.memset(mask_chunk[0:64, 64:128], NEG).then_inc(s_id, 1)
                own(s_id)
                pool.wait_ge(s_id, 9)

        def clear_sems():
            for s in all_sems:
                nc.gpsimd.sem_clear(s)
            nc.all_engine_barrier()

        clear_sems()

        vec_loaded = sem("vec_loaded")
        w_first, rest_loaded = sem("w_first"), sem("rest_loaded")
        band_masked = sem("band_masked")
        x_loaded = [sem(f"x_loaded{i}") for i in range(4)]
        x_squared = sem("x_squared")
        x_rstd = sem("x_rstd")
        x_normed = sem("x_normed")
        gains_scaled = sem("gains_scaled")
        dve_step, act_step, pool_step = sem("dve_step"), sem("act_step"), sem("pool_step")
        w_loaded = [sem(f"w_loaded{i}") for i in range(3)]
        pj_full, pj_free = sem("pj_full"), sem("pj_free")
        t_full, t_free = sem("t_full"), sem("t_free")
        o_full, o_free = sem("o_full"), sem("o_free")
        s_full = sem("s_full")
        row_max = sem("row_max")
        probs_ready = sem("probs_ready")
        probs_scaled = sem("probs_scaled")
        pv_done = sem("pv_done")
        idx_full, idx_relu, idx_added = sem("idx_full"), sem("idx_relu"), sem("idx_added")
        stats_in, rstd_out = sem("stats_in"), sem("rstd_out")
        stats2_in, rstd2_out = sem("stats2_in"), sem("rstd2_out")
        statsp_in, rstdp_out, past_normed = sem("statsp_in"), sem("rstdp_out"), sem("past_normed")
        qk_ready, roped, normed2, roped2 = sem("qk_ready"), sem("roped"), sem("normed2"), sem("roped2")
        gated, mixed, mix_stored, state_stored = sem("gated"), sem("mixed"), sem("mix_stored"), sem("state_stored")
        forget_in, forget_ln, forget_out = sem("forget_in"), sem("forget_ln"), sem("forget_out")
        forget_wide = sem("forget_wide")
        past_loaded = [sem("past_loaded0"), sem("past_loaded1")]
        side_written, side_loaded = sem("side_written"), sem("side_loaded")
        picked, idx_split = sem("picked"), sem("idx_split")
        idx_rows, ik_stored = sem("idx_rows"), sem("ik_stored")
        q_diag_ready, iq_diag_ready, wsel_ready = (sem("q_diag_ready"),
                                                           sem("iq_diag_ready"), sem("wsel_ready"))
        ot_ready = sem("ot_ready")
        out_w, mix_in, x_in, p_in = sem("out_w"), sem("mix_in"), sem("x_in"), sem("p_in")
        a_full, b_full, c_full = sem("out_full"), sem("gate_full"), sem("ple_full")
        x1_ready, sg_exp, x2_ready, x2_stored = sem("x1_ready"), sem("sg_exp"), sem("x2_ready"), sem("x2_stored")
        xn_ready = sem("xn_ready")

        order = schedule()
        ordinal, pj_use, t_use, o_use = count_uses(order)
        past_dmas, n_states = count_dmas()
        last_use = {}
        for key in order:
            if key[0] in ("proj", "iproj"):
                c = PIECES[key[1]][key[3]][0] if key[0] == "proj" else INDEX_CHUNK
                if next_in_buffer(c):
                    last_use[next_in_buffer(c)] = pj_use[key]

        with nc.Fori(0, DEPTH) as layer:
            with ExitStack() as mem, nc.Block() as block:
                def s1(name, shape, dt=F32):
                    return mem.enter_context(nc.sbuf_tensor(name, shape, dt))
                XS = 4
                xt = s1("xt", [P, XS, DM])
                xn = s1("xn", [P, 2, DM])
                sqj = s1("sqj", [P, DM])
                st1 = s1("st1", [P, 2 * NT])

                @block.sync
                def _(sp):
                    for t in range(NT):
                        if t >= XS:
                            sp.wait_ge(x_normed, t - XS + 1)
                        sp.dma_start(xt[:, t % XS, :], lay(xs, layer)[t]).then_inc(x_loaded[t % XS], 16)
                        if t == 0:
                            for dst, src in ((g_in_c, "g_in"), (g_ple_c, "g_ple"), (g_cq_c, "g_cq")):
                                sp.dma_start(dst[:, :], lay(ins[src], layer)).then_inc(vec_loaded, 16)
                            sp.dma_start(gains[:, :, :], lay(ins["g_qk"], layer).unsqueeze(0)
                                         .to_broadcast([P, 8, HD])).then_inc(vec_loaded, 16)
                            sp.dma_start(g_ckv[:, :], ins["g_ckv"][bass.ds(layer, 1), :]
                                         .to_broadcast([P, CKV])).then_inc(vec_loaded, 16)
                            sp.dma_start(g_rope[:, :, :], lay(ins["g_rope"], layer).unsqueeze(0)
                                         .to_broadcast([P, 2, RR])).then_inc(vec_loaded, 16)
                            sp.dma_start(b_f[:, :], ins["b_f"][bass.ds(layer, 1), :]
                                         .to_broadcast([P, H])).then_inc(vec_loaded, 16)
                    for c in range(2):
                        load_chunk(sp, layer, c, w_first)
                    sp.dma_start(band, lay(ins["bias_p"], layer)).then_inc(w_first, 16)
                    sp.wait_ge(w_first, 5 * 16)
                    sp.wait_ge(vec_loaded, 7 * 16)

                @block.gpsimd
                def _(pool):
                    counts = {}

                    def own(s):
                        counts[s.name] = counts.get(s.name, 0) + 1
                        pool.wait_ge(s, counts[s.name])

                    for t in range(NT):
                        pool.wait_ge(x_squared, t + 1)
                        pool.tensor_scalar(st1[:, NT + t:NT + t + 1], st1[:, t:t + 1], EPS, None,
                                           ALU.add).then_inc(pool_step, 1)
                        own(pool_step)
                        pool.wait_ge(pool_step, t + 1)
                        pool.tensor_tensor(st1[:, NT + t:NT + t + 1], st1[:, NT + t:NT + t + 1],
                                           half[:, 0:1], ALU.pow).then_inc(x_rstd, 1)
                        own(x_rstd)
                    pool.wait_ge(w_first, 5 * 16)
                    pool.memset(band[0:64, :, BAND - 64:BAND], NEG).then_inc(band_masked, 1)
                    own(band_masked)
                    pool.memset(band[64:128, :, 0:64], NEG).then_inc(band_masked, 1)
                    own(band_masked)
                    pool.wait_ge(band_masked, 2)

                @block.scalar
                def _(act):
                    counts = {}

                    def own(s):
                        counts[s.name] = counts.get(s.name, 0) + 1
                        act.wait_ge(s, counts[s.name])

                    def square(t):
                        act.wait_ge(x_loaded[t % XS], 16 * (t // XS + 1))
                        if t:
                            act.wait_ge(x_squared, t)
                        act.activation(sqj[:, :], xt[:, t % XS, :], ACT.Square, scale=DM ** -0.5,
                                       accum_out=st1[:, t:t + 1]).then_inc(x_squared, 1)
                        own(x_squared)
                    square(0)
                    for t in range(NT):
                        if t + 1 < NT:
                            square(t + 1)
                        if t == 0:
                            act.wait_ge(vec_loaded, 7 * 16)
                        for j in range(2):
                            act.wait_ge(t_full, 2 * t + j + 1)
                            for k in range(4):
                                a = act.activation(xn_t[:, 4 * j + k, t * P:(t + 1) * P],
                                                   tb[:, j, k * P:(k + 1) * P], ACT.Copy,
                                                   scale=g_in_c[:, 4 * j + k:4 * j + k + 1])
                            a.then_inc(t_free, 1)
                            own(t_free)

                @block.vector
                def _(dve):
                    counts = {}

                    def own(s):
                        counts[s.name] = counts.get(s.name, 0) + 1
                        dve.wait_ge(s, counts[s.name])

                    dve.wait_ge(vec_loaded, 7 * 16)
                    for i in (0, 2, 4):
                        dve.tensor_scalar(gains[:, i, :], gains[:, i, :], HD ** -0.5, None,
                                          ALU.mult).then_inc(gains_scaled, 1)
                        own(gains_scaled)
                    for t in range(NT):
                        dve.wait_ge(x_rstd, t + 1)
                        if t >= 2:
                            dve.wait_ge(t_full, 2 * (t - 1))
                        dve.tensor_scalar(xn[:, t % 2, :], xt[:, t % XS, :], st1[:, NT + t:NT + t + 1], None,
                                          ALU.mult).then_inc(x_normed, 1)
                        own(x_normed)

                @block.tensor
                def _(pe):
                    for t in range(NT):
                        pe.wait_ge(x_normed, t + 1)
                        for j in range(2):
                            if t:
                                pe.wait_ge(t_free, 2 * t + j - 1)
                            for k in range(4):
                                c = 4 * j + k
                                m = nc.tensor.transpose(tb[:, j, k * P:(k + 1) * P],
                                                        xn[:, t % 2, c * P:(c + 1) * P], ident[:, :])
                            m.then_inc(t_full, 1)
            clear_sems()

            with ExitStack() as mem, nc.Block() as block:
                def s2(name, shape, dt=F32):
                    return mem.enter_context(nc.sbuf_tensor(name, shape, dt))

                kt = s2("kt", [P, 4, 1024])
                vv = s2("vv", [P, TP, GW])
                kt8 = s2("kt8", [P, 3, P])
                v8 = s2("v8", [P, GW])
                kt_all = kt[:, :, :].rearrange("p c n -> p (c n)")

                def past(p, lo, n):
                    return kt_all[:, 2048 * (p % 2) + lo:2048 * (p % 2) + lo + n]

                def kt_past(p, c):
                    return past(p, 512 * c, 512).rearrange("p (b n) -> p b n", b=2)

                def ckv_past(p):
                    return past(p, 1536, 512).rearrange("p (b n) -> p b n", b=2)

                def ik_past(p):
                    return past(p, 1024, 512).rearrange("p (b n) -> p b n", b=2)

                def v_past(g, p, b2, blk):
                    k = 2 * b2 + blk
                    if g == B:
                        return vv[:, 4 + k, :] if p % 2 == 0 else ct[:, k * GW:(k + 1) * GW]
                    return past(p, 512 + k * P, P) if g == C else past(p, 1024 + k * GW, GW)

                def nlf_row(p):
                    return ct[:, 512 * (p % 2):512 * (p % 2) + KEYS8]

                def mask_of(t):
                    if t == 2:
                        return mask2[:, :]
                    return ct[:, mask_at(t):mask_at(t) + keys_of(C, t) // 2].bitcast(BF16)
                qt = s2("qt", [P, 2, 4, P])
                z = s2("z", [P, 1028])
                sq = s2("sq", [P, 512])
                sq2 = s2("sq2", [P, GW])
                qk = s2("qk", [P, 512])
                bq = s2("bq", [P, H, 96])
                bk = s2("bk", [P, H, 96])
                eg = s2("eg", [P, GW])
                gate = s2("gate", [P, 2, GW])
                mixt = s2("mixt", [P, 2, GW])
                probs = s2("probs", [P, 2, 1024])
                pt = s2("pt", [P, 2, 1024])
                lat_t = s2("lat_t", [P, 4, P])
                kr = s2("kr", [P, 2, RR])
                acc = s2("acc", [P, 2, 1024])

                def relu8(x):
                    return acc[:, 1, 512 * (x % 2):512 * (x % 2) + KEYS8]

                mask2 = s2("mask2", [P, 384], BF16)
                iqt = s2("iqt", [P, 2, P])
                ikt = s2("ikt", [P, TP * P])
                ikt8 = s2("ikt8", [P, P])
                iqs = s2("iqs", [P, IH, P])
                iw = s2("iw", [P, 3, IH])
                idxs = s2("idxs", [P, 2, 512])
                iq_diag = idxs[:, 1, :].rearrange("p (c b n) -> p c b n", c=2, b=2)
                zi = idxs[:, 1, 0:296]
                ik4 = s2("ik4", [P, 4, ID])
                top8 = s2("top8", [P, 8])
                iw_rows = s2("iw_rows", [P, NB])
                wsel = s2("wsel", [P, 2, 64])
                q_diag = s2("q_diag", [P, 2, 3, 2, 64])
                v_new = ct[0:NQ, 1024:2048].rearrange("p (k b n) -> p k b n", k=2, b=2)
                kp = s2("kp", [P, GW])
                y8 = kp
                keys_now = [kp, bk[:, :, :].rearrange("p h n -> p (h n)")[:, 0:GW]]
                squares_now = [sq2, bq[:, :, :].rearrange("p h n -> p (h n)")[:, 0:GW]]
                ot8 = s2("ot8", [P, 2, P])
                fl = s2("fl", [P, 7, H])
                ik_whole = ik4[:, :, :].rearrange("p a b -> p (a b)")

                def iq_whole(t, b):
                    return (idxs[:, 0, :], acc[:, t % 2, 0:512])[b]

                lfw = idxs[:, 0, :].rearrange("p (h n) -> p h n", h=H)
                zero_row = idxs[:, 0, 0:KEYS8]
                lf_t = s2("lf_t", [H, P])
                stats = s2("stats", [P, 24])
                rstd = s2("rstd", [P, 24])
                mx = s2("mx", [P, 2])
                nmx = s2("nmx", [P, 2])
                sm = s2("sm", [P, 4])
                rs = s2("rs", [P, 4])
                rt = s2("rt", [P, 2, 5 * 32])

                def v_dst(t):
                    return v8[:, :] if t == 8 else vv[:, t, :]

                @block.sync
                def _(sp):
                    def states(g, t):
                        def put(name, src, row=t):
                            sp.dma_start(lay(outs[name], layer)[row], src).then_inc(state_stored, 16)
                        n = ordinal["nmul", g, t]
                        sp.wait_ge(qk_ready, n)
                        if g in (B, C):
                            sp.wait_ge(roped, ordinal["rope", g, t])
                        sp.wait_ge(pj_free, pj_use["proj", g, t, len(PIECES[g]) - 1])
                        if g == A and t >= 4:
                            put("a_k", qk[:, 256:512], t - 4)
                            put("a_v", v_dst(t), t - 4)
                        if g == B:
                            put("b_ckv", qk[:, 384:512])
                            put("b_kr", kr[:, 1, :])
                        if g == C:
                            put("c_k", qk[:, 256:320])
                            put("c_v", v_dst(t)[:, 0:64])
                        if g == D:
                            put("d_k", qk[:, 256:512])
                            put("d_v", v_dst(t))
                            sp.wait_ge(forget_out, t + 1)
                            put("d_lf", fl[:, 5, :])

                    def side(g):
                        if g == C:
                            sp.wait_ge(idx_rows, NT)
                            sp.dma_start(scratch["iw"], iw[:, 2, :]).then_inc(side_written, 16)
                            sp.wait_ge(side_written, 16)
                            for ih in range(IH):
                                sp.dma_start(iw_rows[ih * NQ:(ih + 1) * NQ, :],
                                             scratch["iw"].rearrange("(b q) i -> i q b", q=NQ)[ih],
                                             allow_slow_non_contiguous=True).then_inc(side_loaded, 16)
                        if g == D:
                            sp.wait_ge(t_free, t_use["tcum", 8])
                            sp.dma_start(scratch["lf"], lf_t[:, :].unsqueeze(1).to_broadcast([H, NQ, P])
                                         ).then_inc(side_written, 16)
                            sp.wait_ge(side_written, 32)

                    def load_pack(g, p):
                        def get(dst, src):
                            sp.dma_start(dst, src).then_inc(past_loaded[p % 2], 16)
                        sp.wait_ge(pv_done, unit(g, 8, max(p - 1, 0)))
                        sp.wait_ge(pj_free, pj_use["proj", g, 8, len(PIECES[g]) - 1])
                        if g == B:
                            sp.wait_ge(pj_free, pj_use["upk", 8])
                        lo, w = {A: (0, 2048), B: (1024, 1024), C: (0, 1536), D: (0, 2048)}[g]
                        get(past(p, lo, w), lay(ins["abcd"[g] + "_past"], layer)[p])
                        if g == D:
                            get(nlf_row(p)[:, 0:PAST], lay(ins["d_lf"], layer)[p])
                            for b2 in range(2):
                                get(nlf_row(p)[64 * b2:64 * b2 + 64, PAST:KEYS8],
                                    scratch["lf"].rearrange("h q (b k) -> b (h q) k", b=NB)[2 * p + b2])
                        for b2 in range(2):
                            b = 2 * p + b2
                            for j in range(2 if g == C else 1):
                                w = 64 if g == C else GW
                                get(v_new[:, p % 2, b2, w * j:w * (j + 1)], v8[b * NQ:(b + 1) * NQ, 0:w])

                    load_chunk(sp, layer, INDEX_CHUNK, rest_loaded)
                    sp.dma_start(w_uq[:, :, :], lay(ins["w_uq"], layer).rearrange("(c p) n -> p c n", p=P)
                                 ).then_inc(rest_loaded, 16)
                    sp.dma_start(w_ukv[:, :], lay(ins["w_ukv"], layer)).then_inc(rest_loaded, 16)
                    sp.dma_start(bias_s[:, :], lay(ins["bias_s"], layer)).then_inc(rest_loaded, 16)
                    for st, *a in order:
                        if st == "states":
                            states(*a)
                        elif st == "side":
                            side(*a)
                        elif st == "load_pack":
                            load_pack(*a)
                        elif st == "load_w":
                            (ci,) = a
                            buf = CHUNKS[ci][2]
                            sp.wait_ge(pj_full, last_use[ci])
                            load_chunk(sp, layer, ci, w_loaded[buf])
                        elif st == "load_out":
                            sp.wait_ge(pj_full, pj_use["proj", D, 8, len(PIECES[D]) - 1])
                            for w, name in ((w_out, "w_out"), (w_gate, "w_gate"), (w_ple, "w_ple")):
                                sp.dma_start(w, lay(ins[name], layer).rearrange("(c p) n -> p c n", p=P)
                                             ).then_inc(out_w, 16)
                        elif st == "irows":
                            (t,) = a
                            sp.wait_ge(pj_free, pj_use["iproj", t])
                            sp.dma_start(lay(outs["c_ik"], layer)[t], zi[:, 256:288]).then_inc(ik_stored, 16)
                        elif st in ("y", "y8"):
                            g, t = a
                            sp.wait_ge(mixed, g * NT + t + 1)
                            sp.dma_start(mixd[t, :, g * GW:(g + 1) * GW], mixt[:, t % 2, :]).then_inc(mix_stored, 16)
                    sp.wait_ge(mix_stored, 16 * len(STEPS))
                    sp.wait_ge(state_stored, 16 * n_states[D, 8])
                    sp.wait_ge(ik_stored, 16 * NT)
                    sp.wait_ge(out_w, 3 * 16)

                @block.tensor
                def _(pe):
                    def turn_bank(key):
                        n = t_use[key]
                        if n > 2:
                            pe.wait_ge(t_free, n - 2)
                        return tb[:, (n - 1) % 2, :]

                    def pj_bank(key):
                        if pj_use[key] > 1:
                            pe.wait_ge(pj_free, pj_use[key] - 1)

                    def o_bank(key):
                        if o_use[key] > 1:
                            pe.wait_ge(o_free, o_use[key] - 1)

                    def turn(b, srcs, rows=P):
                        for j, src in enumerate(srcs):
                            m = nc.tensor.transpose(b[0:rows, j * P:j * P + P], src, ident[:, :])
                        m.then_inc(t_full, 1)

                    def project(g, t, i):
                        ci, col, n = PIECES[g][i] if g is not None else (INDEX_CHUNK, 0, 296)
                        if load_ordinal(ci) and t == 0 and col == 0:
                            pe.wait_ge(w_loaded[CHUNKS[ci][2]], 2 * 16 * load_ordinal(ci))
                        pj_bank(("proj", g, t, i) if g is not None else ("iproj", t))
                        w = chunk_view(ci)
                        for k in range(KC):
                            m = nc.tensor.matmul(pj[:, 0:n], xn_t[:, k, t * P:(t + 1) * P], w[:, k, col:col + n],
                                                 start=k == 0, stop=k == KC - 1)
                        m.then_inc(pj_full, 1)

                    def scores(g, t, h):
                        u = unit(g, t, h)
                        if u >= 2:
                            pe.wait_ge(row_max, u - 1)
                        if h == 0:
                            pe.wait_ge(t_free, t_use[LAST_TURN[g], g, t])
                        lo, n = first_key_tile(g, t) * P, keys_of(g, t)
                        for k0 in range(0, n, 512):
                            k1 = min(k0 + 512, n)
                            diag = k1 == n and (g in (B, D) or g == C and not indexed(t))
                            if g == B:
                                l, r = qt[0:96, t % 2, h, :], kt[0:96, h, lo + k0:lo + k1]
                            else:
                                q0 = 64 * (h % 2)
                                l = qt[q0:q0 + 64, t % 2, h // 2, :]
                                r = kt[q0:q0 + 64, 0 if g == C else h // 2, lo + k0:lo + k1]
                            m = nc.tensor.matmul(sc[:, u % 2, k0:k1], l, r, start=True, stop=not diag)
                            if diag:
                                m = nc.tensor.matmul(sc[:, u % 2, n - P:n], ident_h[:, :],
                                                     (mask_causal if g == D else mask_chunk)[:, :],
                                                     start=False, stop=True)
                        m.then_inc(s_full, 1)

                    def turn_probs(g, t, h):
                        u = unit(g, t, h)
                        pe.wait_ge(probs_ready, u + 1)
                        nk = keys_of(g, t) // P
                        for j in range(-(-nk // 4)):
                            turn(turn_bank(("tp", g, t, h, j)),
                                 [probs[:, u % 2, k * P:(k + 1) * P] for k in range(4 * j, min(nk, 4 * j + 4))])

                    def values(g, t, h):
                        u = unit(g, t, h)
                        if h == 0:
                            o_bank(("pv", g, t))
                        lo, nk = first_key_tile(g, t), keys_of(g, t) // P
                        pe.wait_ge(t_free, t_use["tp", g, t, h, -(-nk // 4) - 1])
                        c0 = 0 if g == C else h * HD
                        for k in range(nk):
                            m = nc.tensor.matmul(ob[:, h * HD:(h + 1) * HD], pt[:, u % 2, k * P:(k + 1) * P],
                                                 vv[:, lo + k, c0:c0 + HD], start=k == 0, stop=k == nk - 1)
                        m.then_inc(pv_done, 1)

                    for st, *a in order:
                        if st == "proj":
                            g, t, i = a
                            project(g, t, i)
                        elif st == "iproj":
                            if a[0] == 0:
                                pe.wait_ge(rest_loaded, 5 * 16)
                            project(None, a[0], 0)
                        elif st == "tlat":
                            (t,) = a
                            pe.wait_ge(qk_ready, ordinal["nmul", B, t])
                            turn(turn_bank(("tlat", t)), [qk[:, j * P:(j + 1) * P] for j in range(4)])
                        elif st == "upq":
                            (t,) = a
                            pe.wait_ge(t_free, t_use["tlat", t])
                            pj_bank(("upq", t))
                            for j in range(3):
                                m = nc.tensor.matmul(pj[:, 0:384], lat_t[:, j, :], w_uq[:, j, :],
                                                     start=j == 0, stop=j == 2)
                            m.then_inc(pj_full, 1)
                        elif st == "upk":
                            (t,) = a
                            pj_bank(("upk", t))
                            nc.tensor.matmul(pj[:, :], lat_t[:, 3, :], w_ukv[:, :], start=True,
                                             stop=True).then_inc(pj_full, 1)
                        elif st == "tqk":
                            g, t = a
                            if g == C:
                                pe.wait_ge(roped, ordinal["rope", C, t])
                            else:
                                pe.wait_ge(qk_ready, ordinal["nmul", g, t])
                            turn(turn_bank(("tqk", g, t)), [qk[:, j * P:(j + 1) * P] for j in range(3 if g == C else 4)])
                        elif st == "tix":
                            t, b = a
                            pe.wait_ge(idx_rows, t + 1)
                            ik4_rows = ik4[:, :, :].rearrange("p a b -> p (a b)")
                            if t == 8:
                                rows = [zi[:, 0:128], zi[:, 128:256], ik4_rows]
                            elif b == index_turns(t) - 1:
                                rows = [ik4_rows]
                            else:
                                rows = [acc[:, t % 2, i * P:(i + 1) * P] for i in range(4 * b, 4 * b + 4)]
                            turn(turn_bank(("tix", t, b)), rows)
                        elif st in ("tq", "tk"):
                            g, t = a
                            pe.wait_ge(roped2, t + 1)
                            src = bq if st == "tq" else bk
                            b = turn_bank((st, g, t))
                            if t < 8:
                                turn(b, [src[:, h, :] for h in range(H)], 96)
                            else:
                                c0 = 0 if st == "tq" else 384
                                turn(b, [z[:, c0 + j * P:c0 + (j + 1) * P] for j in range(3)])
                        elif st == "tcum":
                            (t,) = a
                            b = turn_bank(("tcum", t))
                            if t < 8:
                                pe.wait_ge(forget_wide, t + 1)
                                for h in range(H):
                                    m = nc.tensor.matmul(b[:, h * P:(h + 1) * P], lfw[:, h, :], tri[:, :],
                                                         start=True, stop=True)
                                m.then_inc(t_full, 1)
                            else:
                                pe.wait_ge(forget_out, t + 1)
                                nc.tensor.transpose(b[0:H, 0:P], fl[:, 6, :], ident[:, :]).then_inc(t_full, 1)
                        elif st == "isc":
                            t, i, j = a
                            if (i, j) == (0, 0):
                                pe.wait_ge(idx_split, t + 1)
                            k0, k1 = 512 * j, min(512 * j + 512, keys_of(C, t))
                            nc.tensor.matmul(turn_bank(("isc", t, i, j))[:, 0:k1 - k0],
                                             iqs[:, i, :].bitcast(F32R), ikt[:, k0:k1].bitcast(F32R),
                                             start=True, stop=True).then_inc(t_full, 1)
                        elif st == "sc":
                            scores(*a)
                        elif st == "tp":
                            turn_probs(*a)
                        elif st == "pv":
                            values(*a)
                        elif st == "pj_past":
                            p, b2, blk = a
                            if (b2, blk) == (0, 0):
                                pe.wait_ge(past_loaded[p % 2], 16 * past_dmas[B, p])
                            pj_bank(("pj_past", p, b2, blk))
                            nc.tensor.matmul(pj[:, :], ckv_past(p)[:, b2, blk * P:(blk + 1) * P], w_ukv[:, :],
                                             start=True, stop=True).then_inc(pj_full, 1)
                        elif st == "t_past":
                            p, b2, blk = a
                            pe.wait_ge(past_normed, ordinal["t_past", p, b2, blk])
                            k = keys_now[blk]
                            turn(turn_bank(("t_past", p, b2, blk)), [k[:, 0:P], k[:, P:2 * P]])
                        elif st == "isc8":
                            p, b2 = a
                            x = 2 * p + b2
                            if b2 == 0:
                                pe.wait_ge(row_max, unit(C, 8, p))
                                pe.wait_ge(past_loaded[p % 2], 16 * past_dmas[C, p])
                                pe.wait_ge(iq_diag_ready, p + 1)
                            if x >= 2:
                                pe.wait_ge(idx_relu, x - 1)
                            new = slice((2 * p + b2) * NQ, (2 * p + b2 + 1) * NQ)
                            for k0, k1, r in ((0, PAST, ik_past(p)[:, b2, :]), (PAST, KEYS8, ikt8[:, new])):
                                for c in range(2):
                                    m = nc.tensor.matmul(sc[:, x % 2, k0:k1], iq_diag[:, c, b2, :], r,
                                                         start=c == 0, stop=c == 1)
                            m.then_inc(idx_full, 1)
                        elif st == "score8":
                            (p,) = a
                            o_bank(("score8", p))
                            pe.wait_ge(wsel_ready, p + 1)
                            for b2 in range(2):
                                x = 2 * p + b2
                                pe.wait_ge(idx_relu, x + 1)
                                m = nc.tensor.matmul(ob[64 * b2:64 * b2 + 64, 0:KEYS8], wsel[:, b2, :],
                                                     relu8(x), start=True, stop=True)
                            m.then_inc(o_full, 1)
                        elif st == "sc8":
                            g, p = a
                            u = unit(g, 8, p)
                            pe.wait_ge(row_max, u - 1)
                            pe.wait_ge(q_diag_ready, g * PACKS + p + 1)
                            pe.wait_ge(past_loaded[p % 2], 16 * past_dmas[g, p])
                            if p == 0:
                                pe.wait_ge(t_free, t_use[LAST_TURN[g], g, 8])
                            if g == B:
                                pe.wait_ge(t_free, t_use["t_past", p, 1, 1])
                            for b2 in range(2):
                                new = slice((2 * p + b2) * NQ, (2 * p + b2 + 1) * NQ)
                                nchunk = 3 if g == B else 2
                                for k0, k1 in ((0, PAST), (PAST, KEYS8)):
                                    for c in range(nchunk):
                                        cc = 0 if g == C else c
                                        r = kt_past(p, cc)[:, b2, :] if k0 == 0 else kt8[:, cc, new]
                                        m = nc.tensor.matmul(sc[64 * b2:64 * b2 + 64, u % 2, k0:k1],
                                                             q_diag[:, p % 2, c, b2, :], r,
                                                             start=c == 0, stop=c == nchunk - 1)
                            m.then_inc(s_full, 1)
                        elif st == "tp8":
                            g, p = a
                            u = unit(g, 8, p)
                            pe.wait_ge(probs_scaled, g * PACKS + p + 1)
                            b = turn_bank(("tp8", g, p))
                            for k in range(3):
                                w = P if k < 2 else NQ
                                m = nc.tensor.transpose(b[0:w, k * P:(k + 1) * P],
                                                        probs[:, u % 2, k * P:k * P + w], ident[:, :])
                            m.then_inc(t_full, 1)
                        elif st == "pv8":
                            g, p = a
                            u = unit(g, 8, p)
                            o_bank(("pv8", g, p))
                            pe.wait_ge(t_free, t_use["tp8", g, p])
                            for b2 in range(2):
                                for hp in range(2):
                                    c0 = 0 if g == C else hp * P
                                    for k in range(3):
                                        w = P if k < 2 else NQ
                                        v = v_past(g, p, b2, k)[:, c0:c0 + P] if k < 2 else v_new[:, p % 2, b2, c0:c0 + P]
                                        m = nc.tensor.matmul(ob[:, (2 * b2 + hp) * 64:(2 * b2 + hp + 1) * 64], v,
                                                             pt[0:w, u % 2, k * P + 64 * b2:k * P + 64 * b2 + 64],
                                                             start=k == 0, stop=k == 2)
                            m.then_inc(pv_done, 1)
                        elif st == "y8":
                            g, t = a
                            pe.wait_ge(ot_ready, (H - 1) * PACKS * (g + 1))
                            pe.wait_ge(o_free, o_use["pv8", g, PACKS - 1])
                            turn(turn_bank(("y8", g, t)), [ot8[:, 0, :], ot8[:, 1, :]])

                @block.scalar
                def _(act):
                    counts = {}

                    def own(s):
                        counts[s.name] = counts.get(s.name, 0) + 1
                        act.wait_ge(s, counts[s.name])

                    def link(ins):
                        ins.then_inc(act_step, 1)
                        own(act_step)

                    def copy(dst, src, **kw):
                        return act.activation(dst, src, ACT.Copy, **kw)

                    def turned(key):
                        act.wait_ge(t_full, t_use[key])
                        return tb[:, (t_use[key] - 1) % 2, :]

                    def gate_exp(col):
                        copy(z[:, 768:1024], pj[:, col:col + GW])
                        act.activation(eg[:, :], pj[:, col:col + GW], ACT.Exp, scale=-1.0).then_inc(pj_free, 1)
                        own(pj_free)

                    def evac(g, t, i):
                        n = g * NT + t
                        act.wait_ge(pj_full, pj_use["proj", g, t, i])
                        if n and i == 0:
                            pg, ptile = STEPS[n - 1]
                            act.wait_ge(gated, n)
                            if pg in (B, C):
                                act.wait_ge(roped, ordinal["rope", pg, ptile])
                            act.wait_ge(state_stored, 16 * n_states[pg, ptile])
                            if t == 8 and g:
                                for k in range(2):
                                    act.wait_ge(past_loaded[k], 16 * past_dmas[g - 1, PACKS - 2 + k])
                        if i == 0:
                            w = PIECES[g][0][2]
                            copy(z[:, 0:w], pj[:, 0:w])
                            if g == B:
                                act.activation(sq[:, 0:CQ], pj[:, 0:CQ], ACT.Square, scale=CQ ** -0.5,
                                               accum_out=stats[:, 0:1])
                                act.activation(sq[:, CQ:512], pj[:, CQ:512], ACT.Square, scale=CKV ** -0.5,
                                               accum_out=stats[:, 1:2]).then_inc(pj_free, 1)
                                own(pj_free)
                            else:
                                act.activation(sq[:, 0:w], pj[:, 0:w], ACT.Square,
                                               scale=HD ** -0.5).then_inc(pj_free, 1)
                                own(pj_free)
                        elif g == A:
                            copy(v_dst(t), pj[:, 0:256])
                            gate_exp(256)
                        elif g == B:
                            copy(z[:, 512:544], pj[:, 0:32])
                            act.activation(sq2[:, 0:32], pj[:, 0:32], ACT.Square, scale=RR ** -0.5,
                                           accum_out=stats[:, 2:3])
                            gate_exp(32)
                        elif g == C:
                            copy(v_dst(t)[:, 0:64], pj[:, 0:64])
                            gate_exp(64)
                        elif i == 1:
                            copy(v_dst(t), pj[:, 0:256])
                            copy(z[:, 512:516], pj[:, 256:260]).then_inc(pj_free, 1)
                            own(pj_free)
                        else:
                            gate_exp(0)

                    def heads(x, n=H):
                        return x.rearrange("p (h n) -> p h n", h=n)

                    for st, *a in order:
                        if st == "proj":
                            evac(*a)
                        elif st == "iproj":
                            (t,) = a
                            act.wait_ge(pj_full, pj_use["iproj", t])
                            if t > 2:
                                act.wait_ge(idx_added, index_no(min(t, TP), 0))
                            if t:
                                act.wait_ge(ik_stored, 16 * t)
                                act.wait_ge(idx_rows, t)
                                act.wait_ge(t_full, t_use["tix", t - 1, index_turns(t - 1) - 1])
                            copy(zi, pj[:, 0:296]).then_inc(pj_free, 1)
                            own(pj_free)
                        elif st == "tlat":
                            b = turned(("tlat", *a))
                            for j in range(3):
                                copy(lat_t[:, j, :], b[:, j * P:(j + 1) * P], scale=g_cq_c[:, j:j + 1])
                            copy(lat_t[:, 3, :], b[:, 3 * P:4 * P]).then_inc(t_free, 1)
                            own(t_free)
                        elif st == "upq":
                            act.wait_ge(pj_full, pj_use["upq", a[0]])
                            pv, sv = heads(pj[:, 0:384]), heads(sq[:, 0:384])
                            copy(bq[:, :, :], pv)
                            act.activation(sv[:, :, 0:64], pv[:, :, 0:64], ACT.Square, scale=HD ** -0.5)
                            act.activation(sv[:, :, 64:96], pv[:, :, 64:96], ACT.Square,
                                           scale=RR ** -0.5).then_inc(pj_free, 1)
                            own(pj_free)
                        elif st == "upk":
                            (t,) = a
                            act.wait_ge(pj_full, pj_use["upk", t])
                            pv = heads(pj[:, :])
                            copy(bk[:, :, 0:64], pv[:, :, 0:64])
                            copy(heads(v_dst(t)), pv[:, :, 64:128])
                            act.activation(heads(sq2[:, :]), pv[:, :, 0:64], ACT.Square,
                                           scale=HD ** -0.5).then_inc(pj_free, 1)
                            own(pj_free)
                        elif st in ("tq", "tk"):
                            g, t = a
                            b = turned((st, g, t))
                            if t < 8:
                                dst = qt[0:96, t % 2, :, :] if st == "tq" else kt[0:96, :, t * P:(t + 1) * P]
                                copy(dst, heads(b[0:96, :])).then_inc(t_free, 1)
                                own(t_free)
                            else:
                                copy(qt[:, 0, 0:3, :] if st == "tq" else kt8[:, :, :],
                                     heads(b[:, 0:3 * P], 3)).then_inc(t_free, 1)
                                own(t_free)
                        elif st == "tqk":
                            g, t = a
                            b = heads(turned((st, g, t)))
                            copy(qt[:, t % 2, 0:2, :], b[:, 0:2, :])
                            nk = 1 if g == C else 2
                            copy(kt8[:, 0:nk, :] if t == 8 else kt[:, 0:nk, t * P:(t + 1) * P],
                                 b[:, 2:2 + nk, :]).then_inc(t_free, 1)
                            own(t_free)
                        elif st == "tix":
                            t, b = a
                            turned_rows = turned((st, t, b))
                            if t == 8:
                                x = heads(turned_rows)
                                copy(iqt[:, :, :], x[:, 0:2, :])
                                copy(ikt8[:, :], x[:, 2, :]).then_inc(t_free, 1)
                                own(t_free)
                            elif b == index_turns(t) - 1:
                                copy(ikt[:, t * P:(t + 1) * P].bitcast(F32R), turned_rows[:, 0:P])
                                copy(ik_whole, turned_rows[:, 0:P]).then_inc(t_free, 1)
                                own(t_free)
                            else:
                                dst = iqs[:, 4 * b:4 * b + 4, :].rearrange("p h n -> p (h n)")
                                copy(dst.bitcast(F32R), turned_rows)
                                copy(iq_whole(t, b)[64:128], turned_rows[64:128, :]).then_inc(t_free, 1)
                                own(t_free)
                        elif st == "forget":
                            (t,) = a
                            act.wait_ge(forget_in, t + 1)
                            link(act.activation(fl[:, 2, :], fl[:, 1, :], ACT.Exp, scale=-1.0))
                            act.activation(fl[:, 3, :], fl[:, 2, :], ACT.Ln, bias=1.0).then_inc(forget_ln, 1)
                            own(forget_ln)
                        elif st == "tcum":
                            (t,) = a
                            b = turned(("tcum", t))
                            if t == 8:
                                copy(lf_t[:, :], b[0:H, 0:P]).then_inc(t_free, 1)
                                own(t_free)
                            else:
                                if t:
                                    act.wait_ge(t_free, t_use["tcum", t - 1])
                                for h in range(H):
                                    dst = nf[:, h, t * P:(t + 1) * P]
                                    if t == 0:
                                        x = copy(dst, b[:, h * P:(h + 1) * P])
                                    else:
                                        x = act.activation(dst, b[:, h * P:(h + 1) * P], ACT.Identity,
                                                           bias=nf[:, h, t * P - 1:t * P])
                                x.then_inc(t_free, 1)
                                own(t_free)
                        elif st == "isc":
                            t, i, j = a
                            x = index_no(t, i, j)
                            w = min(512, keys_of(C, t) - 512 * j)
                            b = turned((st, t, i, j))
                            if x >= 2:
                                act.wait_ge(idx_added, x - 1)
                            if (i, j) == (0, 0):
                                act.wait_ge(ik_stored, 16 * (t + 1))
                            act.activation(idxs[:, x % 2, 0:w], b[:, 0:w], ACT.Relu,
                                           scale=ID ** -0.5).then_inc(t_free, 1)
                            own(t_free)
                        elif st == "isc8":
                            x = 2 * a[0] + a[1]
                            act.wait_ge(idx_full, x + 1)
                            act.activation(relu8(x), sc[:, x % 2, 0:KEYS8], ACT.Relu,
                                           scale=ID ** -0.5).then_inc(idx_relu, 1)
                            own(idx_relu)
                        elif st in ("sm", "sm8"):
                            g, t, h = a if st == "sm" else (a[0], 8, a[1])
                            u = unit(g, t, h)
                            n = keys_of(g, t) if t < 8 else KEYS8
                            act.wait_ge(row_max, u + 1)
                            act.activation(probs[:, u % 2, 0:n], probs[:, u % 2, 0:n], ACT.Exp,
                                           bias=nmx[:, u % 2:u % 2 + 1],
                                           accum_out=sm[:, u % 4:u % 4 + 1]).then_inc(probs_ready, 1)
                            own(probs_ready)
                        elif st == "tp":
                            g, t, h = a
                            u = unit(g, t, h)
                            nk = keys_of(g, t) // P
                            for j in range(-(-nk // 4)):
                                w = min(nk - 4 * j, 4) * P
                                b = turned(("tp", g, t, h, j))
                                copy(pt[:, u % 2, 512 * j:512 * j + w], b[:, 0:w]).then_inc(t_free, 1)
                                own(t_free)
                        elif st == "tp8":
                            g, p = a
                            u = unit(g, 8, p)
                            b = turned(("tp8", g, p))
                            copy(pt[:, u % 2, 0:2 * P], b[:, 0:2 * P])
                            copy(pt[0:NQ, u % 2, 2 * P:3 * P], b[0:NQ, 2 * P:3 * P]).then_inc(t_free, 1)
                            own(t_free)
                        elif st == "pj_past":
                            p, b2, blk = a
                            act.wait_ge(pj_full, pj_use["pj_past", p, b2, blk])
                            pv = heads(pj[:, :])
                            copy(heads(keys_now[blk][:, :]), pv[:, :, 0:64])
                            copy(heads(v_past(B, p, b2, blk)), pv[:, :, 64:128])
                            act.activation(heads(squares_now[blk][:, :]), pv[:, :, 0:64], ACT.Square,
                                           scale=HD ** -0.5).then_inc(pj_free, 1)
                            own(pj_free)
                        elif st == "t_past":
                            p, b2, blk = a
                            b = turned((st, *a))
                            for c in range(2):
                                x = copy(kt_past(p, c)[:, b2, blk * P:(blk + 1) * P], b[:, c * P:(c + 1) * P])
                            x.then_inc(t_free, 1)
                            own(t_free)
                        elif st == "y8":
                            copy(y8[:, :], turned((st, *a))[:, 0:2 * P]).then_inc(t_free, 1)
                            own(t_free)

                @block.vector
                def _(dve):
                    counts = {}

                    def own(s):
                        counts[s.name] = counts.get(s.name, 0) + 1
                        dve.wait_ge(s, counts[s.name])

                    def link(ins):
                        ins.then_inc(dve_step, 1)
                        own(dve_step)

                    def heads(x, n=H):
                        return x.rearrange("p (h n) -> p h n", h=n)

                    def spread(x, n, w):
                        return x.unsqueeze(2).to_broadcast([P, n, w])

                    def gain(i, n):
                        return gains[:, i:i + 1, :].to_broadcast([P, n, HD])

                    def take_tops(x, rounds, rest):
                        for r in range(rounds):
                            link(dve.max(top8[:, :], x))
                            if r == rounds - 1 and rest:
                                link(dve.memset(top8[:, rest:8], TAKEN))
                            link(dve.match_replace(x, top8[:, :], x, TAKEN))

                    for st, *a in order:
                        if st == "nsum":
                            g, t = a
                            dve.wait_ge(pj_free, pj_use["proj", g, t, 0])
                            n = 5 if g == C else 8
                            dve.tensor_reduce(stats[:, 0:n], heads(sq[:, 0:n * HD], n), AX.X,
                                              ALU.add).then_inc(stats_in, 1)
                            own(stats_in)
                        elif st == "nmul":
                            g, t = a
                            n = g * NT + t
                            dve.wait_ge(rstd_out, n + 1)
                            if n:
                                dve.wait_ge(state_stored, 16 * n_states[STEPS[n - 1]])
                            if g in (A, D):
                                link(dve.tensor_tensor(heads(qk[:, :], 8), heads(z[:, 0:512], 8),
                                                       spread(rstd[:, 0:8], 8, HD), ALU.mult))
                                i = 0 if g == A else 4
                                dve.tensor_tensor(heads(qk[:, 0:256]), heads(qk[:, 0:256]), gain(i, 4), ALU.mult)
                                dve.tensor_tensor(heads(qk[:, 256:512]), heads(qk[:, 256:512]), gain(i + 1, 4),
                                                  ALU.mult).then_inc(qk_ready, 1)
                                own(qk_ready)
                            elif g == C:
                                link(dve.tensor_tensor(heads(qk[:, 0:320], 5), heads(z[:, 0:320], 5),
                                                       spread(rstd[:, 0:5], 5, HD), ALU.mult))
                                dve.tensor_tensor(heads(qk[:, 0:256]), heads(qk[:, 0:256]), gain(2, 4), ALU.mult)
                                dve.tensor_tensor(qk[:, 256:320], qk[:, 256:320], gains[:, 3, :],
                                                  ALU.mult).then_inc(qk_ready, 1)
                                own(qk_ready)
                            else:
                                dve.tensor_scalar(qk[:, 0:CQ], z[:, 0:CQ], rstd[:, 0:1], None, ALU.mult)
                                dve.scalar_tensor_tensor(out=kr[:, 0, :], in0=z[:, 512:544], scalar=rstd[:, 2:3],
                                                         in1=g_rope[:, 1, :], op0=ALU.mult, op1=ALU.mult)
                                dve.scalar_tensor_tensor(out=qk[:, CQ:512], in0=z[:, CQ:512], scalar=rstd[:, 1:2],
                                                         in1=g_ckv[:, :], op0=ALU.mult,
                                                         op1=ALU.mult).then_inc(qk_ready, 1)
                                own(qk_ready)
                        elif st == "nsum2":
                            (t,) = a
                            dve.wait_ge(pj_free, pj_use["upk", t])
                            sv = heads(sq[:, 0:384])
                            dve.tensor_reduce(stats[:, 8:12], sv[:, :, 0:64], AX.X, ALU.add)
                            dve.tensor_reduce(stats[:, 12:16], sv[:, :, 64:96], AX.X, ALU.add)
                            dve.tensor_reduce(stats[:, 16:20], heads(sq2[:, :]), AX.X,
                                              ALU.add).then_inc(stats2_in, 1)
                            own(stats2_in)
                        elif st == "nmul2":
                            (t,) = a
                            dve.wait_ge(rstd2_out, t + 1)
                            dve.tensor_tensor(bq[:, :, 0:64], bq[:, :, 0:64], spread(rstd[:, 8:12], 4, HD), ALU.mult)
                            dve.tensor_tensor(bq[:, :, 64:96], bq[:, :, 64:96], spread(rstd[:, 12:16], 4, RR),
                                              ALU.mult)
                            link(dve.tensor_tensor(bk[:, :, 0:64], bk[:, :, 0:64], spread(rstd[:, 16:20], 4, HD),
                                                   ALU.mult))
                            dve.tensor_tensor(bq[:, :, 0:64], bq[:, :, 0:64], gain(6, 4), ALU.mult)
                            dve.tensor_tensor(bk[:, :, 0:64], bk[:, :, 0:64], gain(7, 4), ALU.mult)
                            dve.tensor_tensor(bq[:, :, 64:96], bq[:, :, 64:96],
                                              g_rope[:, 0:1, :].to_broadcast([P, H, RR]),
                                              ALU.mult).then_inc(normed2, 1)
                            own(normed2)
                        elif st == "gate":
                            g, t = a
                            dve.wait_ge(pj_free, pj_use["proj", g, t, len(PIECES[g]) - 1])
                            link(dve.tensor_scalar(eg[:, :], eg[:, :], 1.0, None, ALU.add))
                            link(dve.reciprocal(eg[:, :], eg[:, :]))
                            dve.tensor_tensor(gate[:, (g * NT + t) % 2, :], z[:, 768:1024], eg[:, :],
                                              ALU.mult).then_inc(gated, 1)
                            own(gated)
                        elif st == "forget":
                            (t,) = a
                            dve.wait_ge(pj_free, pj_use["proj", D, t, 1])
                            if t:
                                dve.wait_ge(state_stored, 16 * n_states[D, t - 1])
                            link(dve.tensor_tensor(fl[:, 0, :], z[:, 512:516], b_f[:, :], ALU.add))
                            dve.tensor_scalar(fl[:, 4, :], fl[:, 0, :], 0.0, None, ALU.min)
                            dve.scalar_tensor_tensor(out=fl[:, 1, :], in0=fl[:, 0, :], scalar=-1.0, in1=fl[:, 0, :],
                                                     op0=ALU.mult, op1=ALU.max).then_inc(forget_in, 1)
                            own(forget_in)
                            dve.wait_ge(forget_in, t + 1)
                            dve.wait_ge(forget_ln, t + 1)
                            dve.tensor_tensor(fl[:, 5, :], fl[:, 4, :], fl[:, 3, :], ALU.subtract)
                            dve.tensor_tensor(fl[:, 6, :], fl[:, 3, :], fl[:, 4, :],
                                              ALU.subtract).then_inc(forget_out, 1)
                            own(forget_out)
                        elif st == "isc":
                            t, i, j = a
                            x, k0 = index_no(t, i, j), 512 * j
                            k1 = min(k0 + 512, keys_of(C, t))
                            dve.wait_ge(t_free, t_use["isc", t, i, j])
                            if i:
                                dve.scalar_tensor_tensor(out=acc[:, t % 2, k0:k1], in0=idxs[:, x % 2, 0:k1 - k0],
                                                         scalar=iw[:, t % 2, i:i + 1], in1=acc[:, t % 2, k0:k1],
                                                         op0=ALU.mult, op1=ALU.add).then_inc(idx_added, 1)
                                own(idx_added)
                            else:
                                dve.tensor_scalar(acc[:, t % 2, k0:k1], idxs[:, x % 2, 0:k1 - k0], iw[:, t % 2, i:i + 1],
                                                  None, ALU.mult).then_inc(idx_added, 1)
                                own(idx_added)
                        elif st == "pick":
                            t, r = a
                            n = keys_of(C, t)
                            if r == 0:
                                link(dve.memset(acc[0:64, t % 2, n - 64:n], NEG))
                            take_tops(acc[:, t % 2, 0:n], ROUNDS, 0)
                            if r == TOPK_P // 8 // ROUNDS - 1:
                                dve.tensor_scalar(mask_of(t), acc[:, t % 2, 0:n], TAKEN / 2, NEG, ALU.is_gt,
                                                  ALU.mult).then_inc(picked, 1)
                                own(picked)
                        elif st == "select8":
                            (p,) = a
                            dve.wait_ge(o_full, p + 1)
                            dve.tensor_copy(acc[:, 0, 0:KEYS8], ob[:, 0:KEYS8]).then_inc(o_free, 1)
                            own(o_free)
                            dve.wait_ge(o_free, o_use["score8", p])
                            x = acc[:, 0, 0:KEYS8]
                            take_tops(x, -(-TOPK_S // 8), TOPK_S % 8)
                            link(dve.tensor_scalar(x, x, TAKEN / 2, NEG, ALU.is_gt, ALU.mult))
                        elif st in ("sm", "sm8"):
                            g, t, h = a if st == "sm" else (a[0], 8, a[1])
                            u = unit(g, t, h)
                            n = keys_of(g, t) if t < 8 else KEYS8
                            if (t, g, h) == (8, A, 0):
                                dve.wait_ge(rest_loaded, 5 * 16)
                            if t == 8 and g == D:
                                dve.wait_ge(past_loaded[h % 2], 16 * past_dmas[D, h])
                                row = nlf_row(h)
                                link(dve.tensor_scalar(row[:, 0:PAST], row[:, 0:PAST], -1.0, None, ALU.mult))
                                if h == 0:
                                    dve.wait_ge(t_full, t_use["tcum", 7])
                                    link(dve.memset(zero_row, 0.0))
                                link(dve.tensor_tensor_scan(row, row, zero_row, 0.0, ALU.add, ALU.add))
                                link(dve.tensor_tensor(row[:, PAST:KEYS8], row[:, PAST:KEYS8], mask_new[:, :],
                                                       ALU.add))
                            if t < 8 and g == D and h == 0:
                                dve.wait_ge(t_free, t_use["tcum", t])
                            dve.wait_ge(s_full, u + 1)
                            dst, src, m = probs[:, u % 2, 0:n], sc[:, u % 2, 0:n], mx[:, u % 2:u % 2 + 1]
                            if g == B or g == C and not indexed(t):
                                x = dve.tensor_scalar(dst, src, MLA_SCALE if g == B else 1.0, None, ALU.mult, ALU.max, accum_out=m)
                            else:
                                if t == 8:
                                    bias = {A: bias_s[:, :], C: acc[:, 0, 0:KEYS8], D: nlf_row(h)}[g]
                                else:
                                    bias = {A: band[:, h, BAND - n:BAND], C: mask_of(t) if indexed(t) else None,
                                            D: nf[:, h, 0:n]}[g]
                                x = dve.tensor_tensor_reduce(dst, src, bias, 1.0, -3.4e38, ALU.add, ALU.max, m)
                            link(x)
                            dve.tensor_scalar(nmx[:, u % 2:u % 2 + 1], m, -1.0, None, ALU.mult).then_inc(row_max, 1)
                            own(row_max)
                        elif st == "tp8":
                            g, p = a
                            u = unit(g, 8, p)
                            dve.wait_ge(probs_ready, u + 1)
                            link(dve.reciprocal(rs[:, 0:1], sm[:, u % 4:u % 4 + 1]))
                            dve.tensor_scalar(probs[:, u % 2, 0:KEYS8], probs[:, u % 2, 0:KEYS8], rs[:, 0:1], None,
                                              ALU.mult).then_inc(probs_scaled, 1)
                            own(probs_scaled)
                        elif st == "pv8":
                            g, p = a
                            dve.wait_ge(pv_done, unit(g, 8, p) + 1)
                            if p == 0 and g:
                                dve.wait_ge(t_full, t_use["y8", g - 1, 8])
                            for h in range(H):
                                r = 64 * (h % 2)
                                src = ob[r:r + 64, 0:256].rearrange("p (b c n) -> p b c n", b=2, c=2)
                                x = dve.tensor_copy(
                                    ot8[r:r + 64, h // 2, 32 * p:32 * p + 32].rearrange("p (b n) -> p b n", b=2),
                                    src[:, :, h // 2, h * NQ:(h + 1) * NQ])
                                x.then_inc(ot_ready if h < H - 1 else o_free, 1)
                                own(ot_ready if h < H - 1 else o_free)
                        elif st == "y":
                            g, t = a
                            n = g * NT + t
                            dve.wait_ge(probs_ready, unit(g, t, 3) + 1)
                            link(dve.reciprocal(rs[:, :], sm[:, :]))
                            dve.wait_ge(pv_done, unit(g, t, 3) + 1)
                            if n:
                                dve.wait_ge(mix_stored, 16 * n)
                            dve.tensor_tensor(heads(mixt[:, t % 2, :]), heads(ob[:, 0:256]), spread(rs[:, :], 4, HD),
                                              ALU.mult).then_inc(o_free, 1)
                            own(o_free)
                            dve.wait_ge(o_free, o_use["pv", g, t])
                            dve.wait_ge(gated, n + 1)
                            dve.tensor_tensor(mixt[:, t % 2, :], mixt[:, t % 2, :], gate[:, (g * NT + t) % 2, :],
                                              ALU.mult).then_inc(mixed, 1)
                            own(mixed)
                        elif st == "y8":
                            g, t = a
                            n = g * NT + t
                            dve.wait_ge(t_free, t_use["y8", g, t])
                            dve.wait_ge(mix_stored, 16 * n)
                            dve.wait_ge(gated, n + 1)
                            dve.tensor_tensor(mixt[:, 0, :], y8[:, :], gate[:, (g * NT + t) % 2, :], ALU.mult).then_inc(mixed, 1)
                            own(mixed)
                        elif st == "pj_past":
                            k = ordinal[("pj_past", *a)]
                            dve.wait_ge(pj_free, pj_use[("pj_past", *a)])
                            dve.tensor_reduce(stats[:, 20:24], heads(squares_now[a[2]][:, :]), AX.X,
                                              ALU.add).then_inc(statsp_in, 1)
                            keys = keys_now[a[2]]
                            own(statsp_in)
                            dve.wait_ge(rstdp_out, k)
                            link(dve.tensor_tensor(heads(keys), heads(keys), spread(rstd[:, 20:24], 4, HD), ALU.mult))
                            dve.tensor_tensor(heads(keys), heads(keys), gain(7, 4),
                                              ALU.mult).then_inc(past_normed, 1)
                            own(past_normed)

                @block.gpsimd
                def _(pool):
                    counts = {}

                    def own(s):
                        counts[s.name] = counts.get(s.name, 0) + 1
                        pool.wait_ge(s, counts[s.name])

                    def link(ins):
                        ins.then_inc(pool_step, 1)
                        own(pool_step)

                    def inv_root(lo, hi):
                        link(pool.tensor_scalar(rstd[:, lo:hi], stats[:, lo:hi], EPS, None, ALU.add))
                        return pool.tensor_tensor(rstd[:, lo:hi], rstd[:, lo:hi], half[:, 0:hi - lo], ALU.pow)

                    def rotate(dst, x, n, w, table, t):
                        c = table[:, 0, t:t + 1, :].to_broadcast([P, n, w])
                        lo, hi = slice(0, w // 2), slice(w // 2, w)
                        s0 = table[:, 1, t:t + 1, lo].to_broadcast([P, n, w // 2])
                        s1 = table[:, 1, t:t + 1, hi].to_broadcast([P, n, w // 2])
                        u = rt[:, 0, 0:n * w].rearrange("p (n w) -> p n w", n=n)
                        v = rt[:, 1, 0:n * w].rearrange("p (n w) -> p n w", n=n)
                        link(pool.tensor_tensor(u, x, c, ALU.mult))
                        link(pool.tensor_tensor(v[:, :, lo], x[:, :, hi], s0, ALU.mult))
                        link(pool.tensor_tensor(v[:, :, hi], x[:, :, lo], s1, ALU.mult))
                        return pool.tensor_tensor(dst, u, v, ALU.add)

                    link(pool.memset(q_diag[:, :, :, :, :], 0.0))
                    for st, *a in order:
                        if st == "rstd":
                            g, t = a
                            if g == B:
                                pool.wait_ge(pj_free, pj_use["proj", B, t, 1])
                                x = inv_root(0, 3)
                            else:
                                pool.wait_ge(stats_in, ordinal["nsum", g, t])
                                x = inv_root(0, 5 if g == C else 8)
                            x.then_inc(rstd_out, 1)
                            own(rstd_out)
                        elif st == "rstd2":
                            pool.wait_ge(stats2_in, a[0] + 1)
                            inv_root(8, 20).then_inc(rstd2_out, 1)
                            own(rstd2_out)
                        elif st == "pj_past":
                            pool.wait_ge(statsp_in, ordinal[("pj_past", *a)])
                            inv_root(20, 24).then_inc(rstdp_out, 1)
                            own(rstdp_out)
                        elif st == "rope":
                            g, t = a
                            pool.wait_ge(qk_ready, ordinal["nmul", g, t])
                            if g == B:
                                rotate(kr[:, 1:2, :], kr[:, 0:1, :], 1, RR, rope_b, t).then_inc(roped, 1)
                                own(roped)
                            else:
                                x = qk[:, 0:320].rearrange("p (h n) -> p h n", h=5)[:, :, 0:16]
                                link(rotate(x, x, 5, 16, rope_c, t))
                                pool.tensor_copy(qk[:, 320:384], qk[:, 256:320]).then_inc(roped, 1)
                                own(roped)
                        elif st == "irows":
                            (t,) = a
                            pool.wait_ge(pj_free, pj_use["iproj", t])
                            if t:
                                pool.wait_ge(t_full, t_use["tix", t - 1, index_turns(t - 1) - 1])
                            if 3 < t < 8:
                                pool.wait_ge(idx_added, index_no(t - 1, 0))
                            if index_turns(t) > 1:
                                if t > 3:
                                    pool.wait_ge(picked, t - 3)
                                link(pool.tensor_copy(acc[:, t % 2, :].rearrange("p (h r n) -> p h r n", h=IH, r=4),
                                                      zi[:, 0:IH * ID].rearrange("p (h n) -> p h n", h=IH).unsqueeze(2)
                                                      .to_broadcast([P, IH, 4, ID])))
                            link(pool.tensor_copy(ik4[:, :, :], zi[:, 256:288].unsqueeze(1).to_broadcast([P, 4, ID])))
                            pool.tensor_scalar(iw[:, 2 if t == 8 else t % 2, :], zi[:, 288:296], IH ** -0.5, None,
                                               ALU.mult).then_inc(idx_rows, 1)
                            own(idx_rows)
                        elif st == "isplit":
                            (t,) = a
                            pool.wait_ge(t_free, t_use["tix", t, index_turns(t) - 1])
                            for b in range(index_turns(t) - 1):
                                x = iqs[64:128, 4 * b:4 * b + 4, :].rearrange("p h n -> p (h n)")
                                link(pool.tensor_tensor(x.bitcast(F32R), iq_whole(t, b)[64:128], x, ALU.subtract))
                            x = ikt[:, t * P:(t + 1) * P]
                            link(pool.tensor_tensor(x[32:64].bitcast(F32R), ik_whole[32:64], x[32:64], ALU.subtract))
                            pool.tensor_tensor(x[96:128].bitcast(F32R), ik_whole[96:128], x[96:128],
                                               ALU.subtract).then_inc(idx_split, 1)
                            own(idx_split)
                        elif st == "rope2":
                            (t,) = a
                            pool.wait_ge(normed2, t + 1)
                            x = bq[:, :, 64:96]
                            link(rotate(x, x, H, RR, rope_b, t))
                            pool.wait_ge(roped, ordinal["rope", B, t])
                            if t < 8:
                                pool.tensor_copy(bk[:, :, 64:96], kr[:, 1:2, :].to_broadcast([P, H, RR])
                                                 ).then_inc(roped2, 1)
                                own(roped2)
                            else:
                                def part(c, n, w):
                                    return z[:, c:c + n * w].rearrange("p (n w) -> p n w", n=n)
                                link(pool.tensor_copy(part(0, H, HD), bq[:, :, 0:HD]))
                                link(pool.tensor_copy(part(256, H, RR), bq[:, :, HD:96]))
                                link(pool.tensor_copy(part(384, H, HD), bk[:, :, 0:HD]))
                                pool.tensor_copy(part(640, H, RR), kr[:, 1:2, :].to_broadcast([P, H, RR])
                                                 ).then_inc(roped2, 1)
                                own(roped2)
                        elif st == "widen":
                            (t,) = a
                            pool.wait_ge(forget_out, t + 1)
                            pool.tensor_copy(lfw[:, :, :], fl[:, 6, :].unsqueeze(2)
                                             .to_broadcast([P, H, P])).then_inc(forget_wide, 1)
                            own(forget_wide)
                        elif st == "q_diag":
                            g, p = a
                            pool.wait_ge(t_free, t_use[LAST_TURN[g], g, 8])
                            if p >= 2:
                                pool.wait_ge(s_full, unit(g, 8, p - 2) + 1)
                            pack = slice(32 * p, 32 * p + 32)
                            parts = []
                            for h in range(H):
                                r = 64 * (h % 2)
                                parts.append((
                                    q_diag[r:r + 64, p % 2, h // 2, :, h * NQ:(h + 1) * NQ],
                                    qt[r:r + 64, 0, h // 2, pack].rearrange("p (b n) -> p b n", b=2)))
                                if g == B:
                                    parts.append((
                                        q_diag[32 * h:32 * h + 32, p % 2, 2, :, h * NQ:(h + 1) * NQ],
                                        qt[32 * h:32 * h + 32, 0, 2, pack].rearrange("p (b n) -> p b n", b=2)))
                            for dst, src in parts[:-1]:
                                link(pool.tensor_copy(dst, src))
                            pool.tensor_copy(*parts[-1]).then_inc(q_diag_ready, 1)
                            own(q_diag_ready)
                        elif st == "iq_diag":
                            (p,) = a
                            if p:
                                pool.wait_ge(idx_full, 2 * p)
                                pool.wait_ge(o_full, p)
                            else:
                                pool.wait_ge(idx_added, index_no(TP, 0))
                                pool.wait_ge(t_free, t_use["tix", 8, 0])
                                link(pool.memset(iq_diag[:, :, :, :], 0.0))
                            for ih in range(IH):
                                r = 32 * (ih % 4)
                                x = pool.tensor_copy(
                                    iq_diag[r:r + 32, ih // 4, :, ih * NQ:(ih + 1) * NQ],
                                    iqt[r:r + 32, ih // 4, 32 * p:32 * p + 32].rearrange("p (b n) -> p b n", b=2))
                                if ih < IH - 1:
                                    link(x)
                            x.then_inc(iq_diag_ready, 1)
                            own(iq_diag_ready)
                            if p == 0:
                                pool.wait_ge(side_loaded, 16 * IH)
                            for b2 in range(2):
                                x = pool.tensor_scalar(wsel[:, b2, :], pick[:, :],
                                                       iw_rows[:, 2 * p + b2:2 * p + b2 + 1], None, ALU.mult)
                            x.then_inc(wsel_ready, 1)
                            own(wsel_ready)
            clear_sems()

            with ExitStack() as mem, nc.Block() as block:
                def s3(name, shape, dt=F32):
                    return mem.enter_context(nc.sbuf_tensor(name, shape, dt))
                SLOTS = 4
                mi = s3("mi", [P, SLOTS, DM])
                xi = s3("xi", [P, SLOTS, DM])
                p_t = s3("p_t", [P, SLOTS, 2, P])
                mi_t = s3("mi_t", [P, KC, P])
                xn3 = s3("xn3", [P, DM])
                xn3_t = s3("xn3_t", [P, KC, P])
                sg = s3("sg", [P, DM])
                st3 = s3("st3", [P, 2 * NT])

                @block.sync
                def _(sp):
                    def load(t):
                        if t >= SLOTS:
                            sp.wait_ge(x2_stored, 16 * (t - SLOTS + 1))
                        sp.dma_start(mi[:, t % SLOTS, :], mixd[t]).then_inc(mix_in, 16)
                        sp.dma_start(xi[:, t % SLOTS, :], lay(xs, layer)[t]).then_inc(x_in, 16)
                        sp.dma_start(p_t[:, t % SLOTS, :, :], lay(ins["p_t"], layer)[t]).then_inc(p_in, 16)
                        sp.wait_ge(mix_in, 16 * (t + 1))
                        sp.wait_ge(x_in, 16 * (t + 1))
                        sp.wait_ge(p_in, 16 * (t + 1))
                    for t in range(SLOTS):
                        load(t)
                    for t in range(NT):
                        sp.wait_ge(x2_ready, t + 1)
                        sp.dma_start(xs[bass.ds(layer + 1, 1), :, :, :].rearrange("a t p n -> (a t) p n")[t],
                                     xi[:, t % SLOTS, :]).then_inc(x2_stored, 16)
                        if t + SLOTS < NT:
                            load(t + SLOTS)
                    sp.wait_ge(x2_stored, 16 * NT)

                turns3 = []
                for t in range(NT + 1):
                    if t < NT:
                        turns3 += [("m", t, 0), ("m", t, 1)]
                    if t >= 1:
                        turns3 += [("x", t - 1, 0), ("x", t - 1, 1)]
                turn3 = {k: i + 1 for i, k in enumerate(turns3)}

                @block.tensor
                def _(pe):
                    def turn(key, src):
                        n = turn3[key]
                        if n > 2:
                            pe.wait_ge(t_free, n - 2)
                        for k in range(4):
                            c = 4 * key[2] + k
                            m = nc.tensor.transpose(tb[:, (n - 1) % 2, k * P:(k + 1) * P], src[:, c * P:(c + 1) * P],
                                                    ident[:, :])
                        m.then_inc(t_full, 1)

                    def product(banks, lhs, w, nk, done):
                        for j in range(2):
                            for k in range(nk):
                                m = nc.tensor.matmul(banks[j], lhs[:, k, :], w[:, k, j * 512:(j + 1) * 512],
                                                     start=k == 0, stop=k == nk - 1)
                        m.then_inc(done, 1)

                    for t in range(NT + 1):
                        if t < NT:
                            pe.wait_ge(mix_in, 16 * (t + 1))
                            for j in range(2):
                                turn(("m", t, j), mi[:, t % SLOTS, :])
                            if t:
                                pe.wait_ge(x1_ready, t)
                            pe.wait_ge(t_free, turn3["m", t, 1])
                            product([sc[:, 0, 0:512], sc[:, 0, 512:1024]], mi_t, w_out, KC, a_full)
                        if t >= 1:
                            s = t - 1
                            if s:
                                pe.wait_ge(x2_ready, s)
                            pe.wait_ge(p_in, 16 * (s + 1))
                            product([pj[:, :], ob[:, :]], p_t[:, s % SLOTS, :, :], w_ple, 2, c_full)
                            pe.wait_ge(xn_ready, s + 1)
                            for j in range(2):
                                turn(("x", s, j), xn3[:, :])
                            pe.wait_ge(t_free, turn3["x", s, 1])
                            if s:
                                pe.wait_ge(sg_exp, s)
                            product([sc[:, 1, 0:512], sc[:, 1, 512:1024]], xn3_t, w_gate, KC, b_full)

                @block.scalar
                def _(act):
                    counts = {}

                    def own(s):
                        counts[s.name] = counts.get(s.name, 0) + 1
                        act.wait_ge(s, counts[s.name])

                    for t in range(NT + 1):
                        if t < NT:
                            for j in range(2):
                                n = turn3["m", t, j]
                                act.wait_ge(t_full, n)
                                if t and j == 0:
                                    act.wait_ge(a_full, t)
                                act.activation(mi_t[:, 4 * j:4 * j + 4, :],
                                               tb[:, (n - 1) % 2, :].rearrange("p (k n) -> p k n", k=4),
                                               ACT.Copy).then_inc(t_free, 1)
                                own(t_free)
                        if t >= 1:
                            s = t - 1
                            for j in range(2):
                                n = turn3["x", s, j]
                                act.wait_ge(t_full, n)
                                for k in range(4):
                                    c = 4 * j + k
                                    a = act.activation(xn3_t[:, c, :], tb[:, (n - 1) % 2, k * P:(k + 1) * P], ACT.Copy,
                                                       scale=g_ple_c[:, c:c + 1])
                                a.then_inc(t_free, 1)
                                own(t_free)
                            if s:
                                act.wait_ge(x2_ready, s)
                            act.wait_ge(b_full, s + 1)
                            act.activation(sg[:, :], sc[:, 1, :], ACT.Exp, scale=-1.0).then_inc(sg_exp, 1)
                            own(sg_exp)

                @block.gpsimd
                def _(pool):
                    counts = {}

                    def own(s):
                        counts[s.name] = counts.get(s.name, 0) + 1
                        pool.wait_ge(s, counts[s.name])

                    for t in range(NT):
                        pool.wait_ge(x_squared, t + 1)
                        pool.tensor_scalar(st3[:, NT + t:NT + t + 1], st3[:, t:t + 1], EPS, None,
                                           ALU.add).then_inc(pool_step, 1)
                        own(pool_step)
                        pool.wait_ge(pool_step, t + 1)
                        pool.tensor_tensor(st3[:, NT + t:NT + t + 1], st3[:, NT + t:NT + t + 1],
                                           half[:, 0:1], ALU.pow).then_inc(x_rstd, 1)
                        own(x_rstd)

                @block.vector
                def _(dve):
                    counts = {}

                    def own(s):
                        counts[s.name] = counts.get(s.name, 0) + 1
                        dve.wait_ge(s, counts[s.name])

                    def link(ins):
                        ins.then_inc(dve_step, 1)
                        own(dve_step)

                    for t in range(NT + 1):
                        if t < NT:
                            dve.wait_ge(a_full, t + 1)
                            dve.wait_ge(x_in, 16 * (t + 1))
                            dve.tensor_tensor(xi[:, t % SLOTS, :], xi[:, t % SLOTS, :], sc[:, 0, :],
                                              ALU.add).then_inc(x1_ready, 1)
                            own(x1_ready)
                            dve.wait_ge(x1_ready, t + 1)
                            if t:
                                dve.wait_ge(t_full, turn3["x", t - 1, 1])
                            dve.scalar_tensor_tensor(out=xn3[:, :], in0=xi[:, t % SLOTS, :], scalar=1.0 / DM,
                                                     in1=xi[:, t % SLOTS, :], op0=ALU.mult, op1=ALU.mult,
                                                     accum_out=st3[:, t:t + 1]).then_inc(x_squared, 1)
                            own(x_squared)
                        if t >= 1:
                            s = t - 1
                            dve.wait_ge(sg_exp, s + 1)
                            link(dve.tensor_scalar(sg[:, :], sg[:, :], 1.0, None, ALU.add))
                            link(dve.reciprocal(sg[:, :], sg[:, :]))
                            dve.wait_ge(c_full, s + 1)
                            dve.tensor_tensor(sg[:, 0:512], sg[:, 0:512], pj[:, :], ALU.mult)
                            link(dve.tensor_tensor(sg[:, 512:1024], sg[:, 512:1024], ob[:, :], ALU.mult))
                            dve.tensor_tensor(xi[:, s % SLOTS, :], xi[:, s % SLOTS, :], sg[:, :],
                                              ALU.add).then_inc(x2_ready, 1)
                            own(x2_ready)
                        if t < NT:
                            dve.wait_ge(x_rstd, t + 1)
                            dve.tensor_scalar(xn3[:, :], xi[:, t % SLOTS, :], st3[:, NT + t:NT + t + 1], None,
                                              ALU.mult).then_inc(xn_ready, 1)
                            own(xn_ready)
            clear_sems()


def kernel(**inputs):
    import numpy as np
    import concourse.bacc as bacc
    from concourse.bass_utils import run_bass_kernel_spmd

    f32 = np.float32
    a = {k: np.asarray(v) for k, v in inputs.items()}
    L = DEPTH

    def rows(prompt, sample):
        lead = prompt.shape[:-3]
        w = prompt.shape[-1]
        return np.concatenate([prompt.reshape(lead + (TP, P, w)), sample.reshape(lead + (1, P, w))], axis=-3)

    pos = np.concatenate([np.arange(TP * P), PAST + np.tile(np.arange(NQ), NB)]).reshape(NT, P)

    def rope(width):
        n = width // 2
        inv = f32(500000.0) ** (-np.arange(n, dtype=f32) / f32(n))
        ang = pos.astype(f32)[:, :, None] * inv[None, None, :]
        c, s = np.cos(ang), np.sin(ang)
        both = np.stack([np.concatenate([c, c], -1), np.concatenate([-s, s], -1)])
        return np.ascontiguousarray(both.transpose(2, 0, 1, 3)).astype(f32)

    i, w = np.arange(P)[:, None], np.arange(BAND)[None, :]
    rel_p = np.clip(i + 512 - w, -128, 128) + 128
    q, k = np.arange(NQ)[:, None], np.arange(KEYS8)[None, :]
    rel_s = np.clip(q + PAST - k, -128, 128) + 128
    rb = a["a_rel_bias"]
    new = np.where(np.arange(NQ)[None, :] > np.arange(NQ)[:, None], f32(NEG), f32(0.0)).astype(f32)
    t = lambda x, *axes: x.transpose(*axes)
    def by_rows(v):
        w = v.shape[-1]
        return v.reshape(L, PACKS, 2, 2, P, w).transpose(0, 1, 4, 2, 3, 5)

    def by_columns(k, times):
        return np.tile(k.reshape(L, PACKS, 2, PAST, -1).transpose(0, 1, 4, 2, 3), (1, 1, times, 1, 1))

    def pack(*parts):
        return np.concatenate([x.reshape(L, PACKS, P, -1) for x in parts], axis=-1)

    def wide(k):
        return k.reshape(L, PACKS, 2, PAST, 2, P).transpose(0, 1, 5, 4, 2, 3)

    past = {
        "a_past": pack(wide(a["cache_a_k"]), by_rows(a["cache_a_v"].reshape(L, NB, PAST, GW))),
        "b_past": pack(by_columns(a["cache_b_krope"], 4), by_columns(a["cache_b_ckv"], 1)),
        "c_past": pack(by_columns(a["cache_c_k"], 2), np.tile(by_rows(a["cache_c_v"]), (1,) * 5 + (2,)),
                       by_columns(a["cache_c_idx_k"], 4)),
        "d_past": pack(wide(a["cache_d_k"]), by_rows(a["cache_d_v"].reshape(L, NB, PAST, GW))),
        "d_lf": np.repeat(a["cache_d_logf"].transpose(0, 1, 3, 2), NQ, axis=2).reshape(L, PACKS, P, PAST),
    }
    ins = {
        "x0": rows(a["x_prompt"][None], a["x_sample"][None])[0],
        "tri": np.triu(np.ones((P, P), f32)),
        "mask_new": np.tile(new, (8, 1)),
        "pick": np.tile(np.eye(NQ, dtype=f32), (IH, H)),
        "rope_b": rope(RR), "rope_c": rope(16),
        "g_in": t(a["g_in"].reshape(L, KC, P), 0, 2, 1),
        "g_ple": t(a["g_ple"].reshape(L, KC, P), 0, 2, 1),
        "g_cq": t(a["b_g_cq"].reshape(L, 3, P), 0, 2, 1),
        "g_qk": a["g_qk"], "g_ckv": a["b_g_ckv"], "g_rope": a["g_rope"], "b_f": a["d_b_f"],
        "w_in": a["w_in"], "w_uq": a["b_w_uq"], "w_ukv": a["b_w_ukv"],
        "w_out": a["w_out"], "w_gate": a["w_ple_gate"], "w_ple": a["w_ple_proj"],
        "bias_p": t(rb[:, :, rel_p], 0, 2, 1, 3),
        "bias_s": np.tile(rb[:, :, rel_s].reshape(L, H * NQ, KEYS8), (1, 2, 1)),
        "p_t": t(rows(a["p_prompt"], a["p_sample"][:, None]).reshape(L, NT, P, 2, P), 0, 1, 4, 3, 2),
        **past,
    }
    ins = {k: np.ascontiguousarray(v) for k, v in ins.items()}
    outs = {"xs": (L + 1, NT, P, DM), "a_k": (L, 5, P, GW), "a_v": (L, 5, P, GW), "b_ckv": (L, NT, P, CKV),
            "b_kr": (L, NT, P, RR), "c_k": (L, NT, P, HD), "c_v": (L, NT, P, HD), "c_ik": (L, NT, P, ID),
            "d_k": (L, NT, P, GW), "d_v": (L, NT, P, GW), "d_lf": (L, NT, P, H)}
    nc = bacc.Bacc("TRN2", target_bir_lowering=False, num_devices=1)
    din = {k: nc.dram_tensor("in_" + k, v.shape, F32, kind="ExternalInput").ap() for k, v in ins.items()}
    dout = {k: nc.dram_tensor("out_" + k, s, F32, kind="ExternalOutput").ap() for k, s in outs.items()}
    scratch = {"xs": dout["xs"],
               "mix": nc.dram_tensor("mix_scratch", (NT, P, DM), F32, kind="Internal").ap(),
               "iw": nc.dram_tensor("iw_scratch", (P, IH), F32, kind="Internal").ap(),
               "lf": nc.dram_tensor("lf_scratch", (H, NQ, P), F32, kind="Internal").ap()}
    build(nc, din, dout, scratch)
    r = run_bass_kernel_spmd(nc, [{"in_" + k: v for k, v in ins.items()}], core_ids=[0]).results[0]
    o = {k: r["out_" + k] for k in outs}

    def prompt(name, tail):
        x = o[name][:, :-1]
        return x.reshape((L, 1, x.shape[1] * P) + tail)

    def sample(name, tail):
        return o[name][:, -1].reshape((L, NB, NQ) + tail)

    tails = [("a_k", (H, HD)), ("a_v", (H, HD)), ("b_ckv", (CKV,)), ("b_kr", (RR,)), ("c_k", (HD,)), ("c_v", (HD,)),
             ("c_ik", (ID,)), ("d_k", (H, HD)), ("d_v", (H, HD)), ("d_lf", (H,))]
    return (o["xs"][L, :TP].reshape(1, TP * P, DM), o["xs"][L, TP].reshape(NB, NQ, DM),
            *[prompt(n, s) for n, s in tails], *[sample(n, s) for n, s in tails])
```
